# Optimizing a Trainium2 kernel written in Bass

```python
import math
import jax, jax.numpy as jnp
from jax import lax
import numpy as np

D_MODEL = 1024
BATCH = 1
SEQ = 2048
DEPTH = 1

CHUNK = 64
MIX_WIDTH = D_MODEL
ATTN_WIDTH = MIX_WIDTH // 2
SGU_WIDTH = MIX_WIDTH - ATTN_WIDTH
HEAD_DIM = 64
N_HEADS = ATTN_WIDTH // HEAD_DIM
KV_HEADS = 2
GQA_GROUP = N_HEADS // KV_HEADS
WINDOW = 128
WINDOW_CHUNKS = WINDOW // CHUNK
ROPE_THETA = 10000.0
SGU_BLOCK = 128
SGU_GROUPS = 4
SGU_GROUP_DIM = SGU_WIDTH // SGU_GROUPS
Q_DIM = N_HEADS * HEAD_DIM
KV_DIM = KV_HEADS * HEAD_DIM
IN_DIM = Q_DIM + 2 * KV_DIM + 2 * SGU_WIDTH
D_FF = int(math.ceil((8 * D_MODEL / 3) / 256) * 256)
NORM_EPS = 1e-6
NEG_INF = -1e30

kernel_name = "hymba_swa_sink_gmlp_sandwich_block"

def rms_norm(x, g):
    xf = x.astype(jnp.float32)
    y = xf * lax.rsqrt(jnp.mean(xf * xf, axis=-1, keepdims=True) + NORM_EPS)
    return (y * g.astype(jnp.float32)).astype(x.dtype)

def layer_norm(x, g, b):
    xf = x.astype(jnp.float32)
    mu = jnp.mean(xf, axis=-1, keepdims=True)
    var = jnp.mean(jnp.square(xf - mu), axis=-1, keepdims=True)
    y = (xf - mu) * lax.rsqrt(var + NORM_EPS)
    return (y * g.astype(jnp.float32) + b.astype(jnp.float32)).astype(x.dtype)

def rope_tables(seq_len, dtype):
    inv_freq = 1.0 / (ROPE_THETA ** (jnp.arange(0, HEAD_DIM, 2, dtype=jnp.float32) / HEAD_DIM))
    pos = jnp.arange(seq_len, dtype=jnp.float32)
    ang = pos[:, None] * inv_freq[None, :]
    return jnp.cos(ang).astype(dtype), jnp.sin(ang).astype(dtype)

def apply_rope(t, cos, sin):
    t1, t2 = jnp.split(t, 2, axis=-1)
    c = cos[None, :, None, :]
    s = sin[None, :, None, :]
    return jnp.concatenate([t1 * c - t2 * s, t2 * c + t1 * s], axis=-1)

def chunk_window(t):
    parts = []
    for s in range(WINDOW_CHUNKS - 1, -1, -1):
        if s == 0:
            parts.append(t)
        else:
            shifted = jnp.pad(t, ((0, 0), (s, 0), (0, 0), (0, 0), (0, 0)))[:, :-s]
            parts.append(shifted)
    return jnp.concatenate(parts, axis=2)

def window_sink_attention(q, k, v, sinks):
    B, S = q.shape[0], q.shape[1]
    n_chunks = S // CHUNK
    W = WINDOW_CHUNKS * CHUNK
    qc = q.reshape(B, n_chunks, CHUNK, KV_HEADS, GQA_GROUP, HEAD_DIM)
    kw = chunk_window(k.reshape(B, n_chunks, CHUNK, KV_HEADS, HEAD_DIM))
    vw = chunk_window(v.reshape(B, n_chunks, CHUNK, KV_HEADS, HEAD_DIM))
    scale = 1.0 / math.sqrt(HEAD_DIM)
    scores = jnp.einsum('bnqkgd,bnjkd->bnkgqj', qc, kw).astype(jnp.float32) * scale
    key_chunk = jnp.arange(n_chunks)[:, None] - (WINDOW_CHUNKS - 1 - jnp.arange(W) // CHUNK)[None, :]
    valid = (key_chunk >= 0)[None, :, None, None, None, :]
    scores = jnp.where(valid, scores, NEG_INF)
    sink = jnp.broadcast_to(
        sinks.astype(jnp.float32).reshape(KV_HEADS, GQA_GROUP)[None, None, :, :, None, None],
        scores.shape[:-1] + (1,))
    probs = jax.nn.softmax(jnp.concatenate([scores, sink], axis=-1), axis=-1)[..., :-1]
    out = jnp.einsum('bnkgqj,bnjkd->bnqkgd', probs.astype(v.dtype), vw)
    return out.reshape(B, S, N_HEADS * HEAD_DIM)

def spatial_gating(u, v, ln_g, ln_b, w_s, b_s):
    B, S = u.shape[0], u.shape[1]
    n_blocks = S // SGU_BLOCK
    vn = layer_norm(v, ln_g, ln_b).reshape(B, n_blocks, SGU_BLOCK, SGU_GROUPS, SGU_GROUP_DIM)
    pos_chunk = jnp.arange(SGU_BLOCK) // CHUNK
    mask = (pos_chunk[:, None] >= pos_chunk[None, :]).astype(w_s.dtype)
    w_masked = w_s * mask[None]
    gate = jnp.einsum('gij,bnjgc->bnigc', w_masked, vn) + jnp.transpose(b_s)[None, None, :, :, None]
    return u * gate.reshape(B, S, SGU_WIDTH)

def swiglu(h, w_gate, w_up, w_down):
    return (jax.nn.silu(h @ w_gate) * (h @ w_up)) @ w_down

def setup_inputs(seed: int = 0) -> dict:
    key = jax.random.key(seed)
    ks = jax.random.split(key, 18)
    f32 = jnp.float32

    def gain(k, n):
        return 1.0 + 0.05 * jax.random.normal(k, (DEPTH, n), f32)

    return {
        "x": jax.random.normal(ks[0], (BATCH, SEQ, D_MODEL), f32),
        "norm_mix_pre": gain(ks[1], D_MODEL),
        "norm_mix_post": gain(ks[2], D_MODEL),
        "w_in": jax.random.normal(ks[3], (DEPTH, D_MODEL, IN_DIM), f32) * D_MODEL ** -0.5,
        "attn_sinks": 0.5 * jax.random.normal(ks[4], (DEPTH, N_HEADS), f32),
        "sgu_ln_g": gain(ks[5], SGU_WIDTH),
        "sgu_ln_b": 0.02 * jax.random.normal(ks[6], (DEPTH, SGU_WIDTH), f32),
        "sgu_w": jax.random.normal(ks[7], (DEPTH, SGU_GROUPS, SGU_BLOCK, SGU_BLOCK), f32) * SGU_BLOCK ** -0.5,
        "sgu_b": 1.0 + 0.1 * jax.random.normal(ks[8], (DEPTH, SGU_GROUPS, SGU_BLOCK), f32),
        "norm_out_attn": gain(ks[9], ATTN_WIDTH),
        "norm_out_sgu": gain(ks[10], SGU_WIDTH),
        "w_out": jax.random.normal(ks[11], (DEPTH, MIX_WIDTH, D_MODEL), f32) * MIX_WIDTH ** -0.5,
        "norm_ffn_pre": gain(ks[12], D_MODEL),
        "norm_ffn_post": gain(ks[13], D_MODEL),
        "w_gate": jax.random.normal(ks[14], (DEPTH, D_MODEL, D_FF), f32) * D_MODEL ** -0.5,
        "w_up": jax.random.normal(ks[15], (DEPTH, D_MODEL, D_FF), f32) * D_MODEL ** -0.5,
        "w_down": jax.random.normal(ks[16], (DEPTH, D_FF, D_MODEL), f32) * D_FF ** -0.5,
    }

def reference(x, norm_mix_pre, norm_mix_post, w_in, attn_sinks, sgu_ln_g, sgu_ln_b,
              sgu_w, sgu_b, norm_out_attn, norm_out_sgu, w_out, norm_ffn_pre,
              norm_ffn_post, w_gate, w_up, w_down):
    B, S, _ = x.shape
    cos, sin = rope_tables(S, x.dtype)
    for l in range(DEPTH):
        h = rms_norm(x, norm_mix_pre[l])
        z = h @ w_in[l]
        o1 = Q_DIM
        o2 = o1 + KV_DIM
        o3 = o2 + KV_DIM
        o4 = o3 + SGU_WIDTH
        q = apply_rope(z[..., :o1].reshape(B, S, N_HEADS, HEAD_DIM), cos, sin)
        k = apply_rope(z[..., o1:o2].reshape(B, S, KV_HEADS, HEAD_DIM), cos, sin)
        v = z[..., o2:o3].reshape(B, S, KV_HEADS, HEAD_DIM)
        a_out = window_sink_attention(q, k, v, attn_sinks[l])
        g_in = jax.nn.gelu(z[..., o3:], approximate=False)
        s_out = spatial_gating(g_in[..., :SGU_WIDTH], g_in[..., SGU_WIDTH:],
                               sgu_ln_g[l], sgu_ln_b[l], sgu_w[l], sgu_b[l])
        mix = jnp.concatenate([rms_norm(a_out, norm_out_attn[l]),
                               rms_norm(s_out, norm_out_sgu[l])], axis=-1) @ w_out[l]
        x = x + rms_norm(mix, norm_mix_post[l])
        f = swiglu(rms_norm(x, norm_ffn_pre[l]), w_gate[l], w_up[l], w_down[l])
        x = x + rms_norm(f, norm_ffn_post[l])
    return x


_drawn_inputs = setup_inputs


def setup_inputs(seed=0):
    import zlib

    import numpy as np

    out = dict(_drawn_inputs(seed))
    spreads = {}
    factors = {'attn_sinks': 8.0, 'sgu_ln_g': 3.015, 'sgu_ln_b': 7.019}
    for name, (base, spread) in spreads.items():
        noise = np.random.default_rng([zlib.crc32(name.encode()), seed]).standard_normal(out[name].shape)
        drawn = base * np.exp(spread * noise) if base else spread * noise
        out[name] = __import__('jax').numpy.asarray(drawn.astype(out[name].dtype))
    for name, factor in factors.items():
        out[name] = (out[name] * factor).astype(out[name].dtype)
    return out
```

```python
import numpy as np

import concourse.bass as bass
from concourse import mybir

F32 = mybir.dt.float32
F32R = mybir.dt.float32r
BF16 = mybir.dt.bfloat16
ALU = mybir.AluOpType
ACT = mybir.ActivationFunctionType
AX_X = mybir.AxisListType.X

P = 128
SEQ, D = 2048, 1024
KD = D // P
TILES = SEQ // P
HD, NH, KVH = 64, 8, 2
PAIRS = NH // KVH
AW = NH * HD
SW = 512
SG = SW // P
CH = 64
WIN = AW + 2 * KVH * HD + 2 * SW
DFF = 2816
BLK = 1024
NB = SEQ // BLK
BT = BLK // P
GW = 256
NG = DFF // GW
EPS = 1e-6
NEG = -1e30


def build_kernel(nc, x, w_in, w_out, w_gate, w_up, w_down, gain_in, gain_out, post_mix, pre_ffn,
                 post_ffn, sinks, ln_g, ln_b, sgu_wt, sgu_bt, rope, out):
    mix_d = nc.dram_tensor("mix_d", (SEQ, D), F32).ap()
    x1_d = nc.dram_tensor("x1_d", (SEQ, D), F32).ap()
    h2_d = nc.dram_tensor("h2_d", (P, 2, KD, SEQ), F32).ap()

    KB = 1024
    START = 16512

    def at(name, kb, shape, dt=F32):
        return nc.alloc_sbuf_tensor_at(name, [P] + list(shape), dt, offset=START + int(kb * KB))

    win_hi = at("win_hi", 90, [KD, WIN], F32R)
    win_lo = at("win_lo", 146, [KD, WIN], F32R)
    wraw = [at(f"wraw{i}", 10 + 4 * i, [2 * SW]) for i in range(3)]
    ropeA = at("ropeA", 0, [AW + P])
    ropeB = at("ropeB", 2.5, [AW + P])
    qT = at("qT", 5, [AW])
    kA = [at(f"kA{i}", 7 + 0.5 * i, [P]) for i in range(2)]
    kB = at("kB", 8, [P])
    vA = [at(f"vA{i}", 8.5 + 0.5 * i, [P]) for i in range(2)]
    vB = at("vB", 9.5, [P])
    probs = at("probs", 10, [NH * P])
    probsT = at("probsT", 14, [NH * P])
    gel = at("gel", 18, [2 * SW])
    vhat = at("vhat", 22, [SW])
    vn1 = at("vn1", 24, [SW])
    vn = at("vn", 26, [SW])
    sB = at("sB", 28, [SW])
    aO = at("aO", 30, [AW])
    hT_hi = [at(f"hT_hi{i}", 32 + 4 * i, [D], F32R) for i in range(2)]
    hT_lo = [at(f"hT_lo{i}", 40 + 4 * i, [D], F32R) for i in range(2)]
    xt = [at(f"xt{i}", 48 + 4 * i, [D]) for i in range(2)]
    xn = at("xn", 56, [D])
    qrot = at("qrot", 60, [AW])
    krot = at("krot", 62, [P])
    mix = [at(f"mix{i}", 64 + 4 * i, [D]) for i in range(2)]
    cs = at("cs", 72, [TILES, 96])
    lng = at("lng", 78, [SW])
    lnb = at("lnb", 80, [SW])
    squares1 = at("squares1", 82, [D], BF16)

    wout_raw = [at(f"wout_raw{c}", 92 + 4 * c if c < 5 else 156 + 4 * c, [D]) for c in range(KD)]
    wout_hi = at("wout_hi", 112, [KD, D], F32R)
    wout_lo = at("wout_lo", 144, [KD, D], F32R)
    mixT_hi = [at(f"mixT_hi{i}", 32 + 4 * i, [D], F32R) for i in range(2)]
    mixT_lo = [at(f"mixT_lo{i}", 40 + 4 * i, [D], F32R) for i in range(2)]
    mixin = [at(f"mixin{i}", 48 + 4 * i, [D]) for i in range(2)]
    xres = [at(f"xres{i}", 56 + 4 * i, [D]) for i in range(2)]
    ytmp = at("ytmp", 176, [D])
    h2s = at("h2s", 180, [2, KD, P], F32R)
    h2s_end = at("h2s_end", 168, [2, KD, P], F32R)
    postm = at("postm", 188, [D])
    pref = at("pref", 192, [D])
    h2n = at("h2n", 196, [D])
    squares2 = at("squares2", 200, [D], BF16)

    h2T_hi = [at(f"h2T_hi{h}", 32 * h, [KD, 512], F32R) for h in range(2)]
    h2T_lo = [at(f"h2T_lo{h}", 32 * h + 16, [KD, 512], F32R) for h in range(2)]
    gu_hi = [at(f"gu_hi{f}", 64 + 8 * f, [2, KD, P], F32R) for f in range(2)]
    gu_lo = [at(f"gu_lo{f}", 80 + 8 * f, [2, KD, P], F32R) for f in range(2)]
    raw_a = at("raw_a", 96, [KD * GW])
    raw_b = at("raw_b", 104, [KD * GW])
    act_hi = at("act_hi", 112, [2, BLK], F32R)
    act_lo = at("act_lo", 120, [2, BLK], F32R)
    wd_hi = at("wd_hi", 128, [2, D], F32R)
    wd_lo = at("wd_lo", 136, [2, D], F32R)
    acc = at("acc", 144, [BT, D])
    th = [at(f"th{i}", 176 + 2 * i, [512]) for i in range(2)]
    sil = [at(f"sil{i}", 180 + 2 * i, [512]) for i in range(2)]
    prod = [at(f"prod{i}", 184 + 2 * i, [512]) for i in range(2)]
    postf = at("postf", 188, [D])
    x1r = [at(f"x1r{i}", 192 + 4 * i, [D]) for i in range(2)]
    squares3 = at("squares3", 200, [D], BF16)

    place = [202.0]

    def small(name, *shape):
        t = at(name, place[0], shape)
        place[0] += (4 * int(np.prod(shape)) + 31) // 32 * 32 / KB
        return t

    ident = small("ident", P)
    gcol_in, gcol_out = small("gcol_in", KD), small("gcol_out", KD)
    mhalf = small("mhalf", 2)
    sgu_w = small("sgu_w", SG, P)
    sgub, sinkb = small("sgub", SG), small("sinkb", NH)
    ssx, msx, rstdx = small("ssx", 2), small("msx", 2), small("rstdx", 2)
    pbias = small("pbias", 1)
    mraw, mtop, mneg, dsink = (small(n, NH) for n in ("mraw", "mtop", "mneg", "dsink"))
    den, esink, dtot, rden = (small(n, NH) for n in ("den", "esink", "dtot", "rden"))
    st6, mv, varm, rstdv = small("st6", 6), small("mv", 2), small("varm", 1), small("rstdv", 1)
    ss2, ms2, rs2 = small("ss2", 2), small("ms2", 2), small("rs2", 2)
    ssm, msm, rstdm = small("ssm", 2), small("msm", 2), small("rstdm", 2)
    ssy, msy, rstdy = small("ssy", 2), small("msy", 2), small("rstdy", 2)
    ssf, msf, rstdf = small("ssf", BT), small("msf", BT), small("rstdf", BT)
    assert START + place[0] * KB <= nc.sbuf_usable_end

    T0 = nc.alloc_psum_tensor("T0", [P, 512], F32)
    T1 = nc.alloc_psum_tensor("T1", [P, 512], F32)
    S = nc.alloc_psum_tensor("S", [P, 2, 512], F32)
    ZA = nc.alloc_psum_tensor("ZA", [P, 2, 512], F32)
    ZB = nc.alloc_psum_tensor("ZB", [P, 2, 512], F32)
    T = [T0, T1]
    M = [ZA, ZB]
    GU = [ZA, ZB]
    DN = [T0[:, :], T1[:, :], S[:, 0, :], S[:, 1, :]]

    sem = nc.alloc_semaphore

    def pair(name):
        return [sem(f"{name}{i}") for i in range(2)]

    gains_in, consts, posts, post_in = sem("gains_in"), sem("consts"), sem("posts"), sem("post_in")
    wraw_in = [sem(f"wraw_in{i}") for i in range(3)]
    win_hi_done, win_split = sem("win_hi_done"), sem("win_split")
    x_in, mix_out = pair("x_in"), pair("mix_out")
    id_zero, pool_consts = sem("id_zero"), sem("pool_consts")
    ssx_done, msx_ready, rstdx_ready, xn_done = sem("ssx_done"), sem("msx_ready"), sem("rstdx_ready"), sem("xn_done")
    t_full, t_drained = pair("t_full"), pair("t_drained")
    h_hi_done, zqkv_full, zu_full, zus_full = sem("h_hi_done"), sem("zqkv_full"), sem("zu_full"), sem("zus_full")
    rope_mul, rot_done, v_done, k_done = sem("rope_mul"), sem("rot_done"), sem("v_done"), sem("k_done")
    gel_done, st6_done, mv_done, var_ready = sem("gel_done"), sem("st6_done"), sem("mv_done"), sem("var_ready")
    rstdv_ready, vhat_done, vn1_done, vn_ready = sem("rstdv_ready"), sem("vhat_done"), sem("vn1_done"), sem("vn_ready")
    s_full, masked, mraw_done = sem("s_full"), sem("masked"), sem("mraw_done")
    mtop_done, soft_ready, exp_done = sem("mtop_done"), sem("soft_ready"), sem("exp_done")
    dtot_done, rden_done, g_full, pv_done = sem("dtot_done"), sem("rden_done"), sem("g_full"), sem("pv_done")
    sB_done, aO_done, ss2_done, ms2_ready = sem("sB_done"), sem("aO_done"), sem("ss2_done"), sem("ms2_ready")
    rs2_ready, mix_done = sem("rs2_ready"), sem("mix_done")
    wout_in = [sem(f"wout_in{c}") for c in range(KD)]
    wout_hi_done, wout_split = sem("wout_hi_done"), sem("wout_split")
    mix_in, xres_in, x1_out, h2_out = pair("mix_in"), pair("xres_in"), pair("x1_out"), sem("h2_out")
    mixT_full, mixT_hi_done, mixT_split, mm2_full = sem("mixT_full"), sem("mixT_hi_done"), sem("mixT_split"), sem("mm2_full")
    ssm_done, msm_ready, rstdm_ready = sem("ssm_done"), sem("msm_ready"), sem("rstdm_ready")
    y_done, x1_done, ssy_done, msy_ready = sem("y_done"), sem("x1_done"), sem("ssy_done"), sem("msy_ready")
    rstdy_ready, h2n_done, h2T_full = sem("rstdy_ready"), sem("h2n_done"), sem("h2T_full")
    h2s_hi_done, h2s_split = sem("h2s_hi_done"), sem("h2s_split")
    h2T_in = pair("h2T_in")
    gate_in, up_in, down_in = sem("gate_in"), sem("up_in"), sem("down_in")
    gu_hi_done, gate_split, up_split = sem("gu_hi_done"), sem("gate_split"), sem("up_split")
    wd_hi_done, wd_split = sem("wd_hi_done"), sem("wd_split")
    gu_full, gu_drained = pair("gu_full"), pair("gu_drained")
    th_done, sil_done, act_hi_done, act_split = sem("th_done"), sem("sil_done"), sem("act_hi_done"), sem("act_split")
    dn_full = [sem(f"dn_full{i}") for i in range(4)]
    acc_added = [sem(f"acc_added{i}") for i in range(4)]
    acc_zero, ssf_done, msf_ready, rstdf_ready = sem("acc_zero"), sem("ssf_done"), sem("msf_ready"), sem("rstdf_ready")
    yf_done, out_done, x1r_in, out_stored = sem("yf_done"), sem("out_done"), pair("x1r_in"), pair("out_stored")
    passed_pe, passed_dve, passed_sp = sem("passed_pe"), sem("passed_dve"), sem("passed_sp")

    def rows(t):
        return bass.ds(t * P, P)

    def flat(ap):
        return ap.rearrange("p a n -> p (a n)")

    def chunk(c):
        return slice(c * P, (c + 1) * P)

    def passed(e, name):
        e.sem_inc(name, 1)

    def add_x1(e, s):
        e.wait_ge(x1r_in[s % 2], 16 * (s // 2 + 1))
        e.wait_ge(yf_done, s + 1)
        e.tensor_tensor(x1r[s % 2][:, :], acc[:, s % BT, :], x1r[s % 2][:, :], ALU.add).then_inc(out_done, 1)

    def use_h(k):
        return 3 * k + 1

    def use_q(k, last):
        return 3 * k + 2 - last

    def use_p(k, last):
        return 3 * k + 3 - last

    def over_tiles(e, body):
        body(0, 0, 0, 0, True)
        body(0, 1, 1, 0, True)
        with e.Fori(1, TILES // 2 - 1) as j:
            for par in range(2):
                body(j, par, 2, 0, True)
        body(TILES // 2 - 1, 0, 2, 0, False)
        body(TILES // 2 - 1, 1, 2, 1, False)

    PIECES = [(c, slice(0, 768)) for c in range(KD)] + [(c, slice(768, WIN)) for c in range(KD)]

    def piece(i):
        c, w = PIECES[i]
        return c, w, wraw[i % 3][:, 0:w.stop - w.start]

    gate_v = w_gate.rearrange("(k p) n -> p k n", p=P)
    up_v = w_up.rearrange("(k p) n -> p k n", p=P)
    down_v = w_down.rearrange("(g f p) n -> g p f n", f=2, p=P)
    gate_raw = raw_a[:, :].rearrange("p (k n) -> p k n", k=KD)
    up_raw = raw_b[:, :].rearrange("p (k n) -> p k n", k=KD)
    down_raw = raw_a[:, :].rearrange("p (f n) -> p f n", f=2)

    block = nc.Block()
    with block:
        @block.sync
        def _(e):
            e.dma_start(xt[0][:, :], x[0:P, :]).then_inc(x_in[0], 16)
            e.dma_start(gcol_in[:, :], gain_in).then_inc(gains_in, 16)
            for i in range(len(PIECES)):
                c, w, raw = piece(i)
                if i >= 3:
                    e.wait_ge(win_split, i - 2)
                e.dma_start(raw, w_in[chunk(c), w]).then_inc(wraw_in[i % 3], 16)
                if i == 1:
                    e.dma_start(xt[1][:, :], x[P:2 * P, :]).then_inc(x_in[1], 16)
                if i == 7:
                    for dst, src in ((cs, rope), (sgu_w, sgu_wt)):
                        e.dma_start(dst[:, :, :], src).then_inc(consts, 16)
                    for dst, src in ((sgub, sgu_bt), (sinkb, sinks), (lng, ln_g), (lnb, ln_b), (gcol_out, gain_out)):
                        e.dma_start(dst[:, :], src).then_inc(consts, 16)
            for m in (2, 3):
                e.wait_ge(xn_done, m - 1)
                e.dma_start(xt[m % 2][:, :], x[m * P:(m + 1) * P, :]).then_inc(x_in[m % 2], 16)

            def tile(k, par, more):
                if more:
                    e.wait_ge(xn_done, k + 3)
                    e.dma_start(xt[par][:, :], x[rows(k + 4), :]).then_inc(x_in[par], 16)
                e.wait_ge(mix_done, 2 * k + 2)
                e.dma_start(mix_d[rows(k), :], mix[par][:, :]).then_inc(mix_out[par], 16)

            with e.Fori(0, TILES // 2 - 2) as j:
                for par in range(2):
                    tile(j * 2 + par, par, True)
            for k in range(TILES - 4, TILES - 1):
                tile(k, k % 2, False)

            e.wait_ge(zus_full, TILES)
            for c in range(KD):
                e.dma_start(wout_raw[c][:, :], w_out[chunk(c), :]).then_inc(wout_in[c], 16)
                if c == 0:
                    e.wait_ge(mix_out[0], 16 * (TILES // 2))
                    e.dma_start(mixin[0][:, :], mix_d[0:P, :]).then_inc(mix_in[0], 16)
            e.dma_start(xres[0][:, :], x[0:P, :]).then_inc(xres_in[0], 16)
            e.dma_start(postm[:, :], post_mix).then_inc(posts, 16)
            e.dma_start(pref[:, :], pre_ffn).then_inc(posts, 16)
            tile(TILES - 1, 1, False)
            e.wait_ge(mix_out[1], 16 * (TILES // 2))
            e.dma_start(mixin[1][:, :], mix_d[P:2 * P, :]).then_inc(mix_in[1], 16)
            e.dma_start(xres[1][:, :], x[P:2 * P, :]).then_inc(xres_in[1], 16)

            def h2_store(k, src=h2s):
                e.wait_ge(h2s_split, 2 * k + 2)
                passed(e, passed_sp)
                for c in range(2):
                    e.dma_start(h2_d[:, c, :, rows(k)], src[:, c, :, :].bitcast(F32)).then_inc(h2_out, 16)

            def tile2(j, par, before, last, ahead):
                k = 2 * j + par
                if ahead:
                    e.wait_ge(mixT_full, 2 * k + 2)
                    e.dma_start(mixin[par][:, :], mix_d[rows(k + 2), :]).then_inc(mix_in[par], 16)
                e.wait_ge(x1_done, k + 1)
                e.dma_start(x1_d[rows(k), :], xres[par][:, :]).then_inc(x1_out[par], 16)
                if before:
                    h2_store(k - 1)
                    if not last:
                        e.wait_ge(h2n_done, k)
                        passed(e, passed_sp)
                        e.wait_ge(x1_out[1 - par], 16 * (j + par))
                        passed(e, passed_sp)
                        e.dma_start(xres[1 - par][:, :], x[rows(k + 1), :]).then_inc(xres_in[1 - par], 16)

            def load_gate_up(n, g):
                if not isinstance(n, int) or n:
                    e.wait_ge(wd_split, n)
                e.dma_start(gate_raw, gate_v[:, :, bass.ds(g * GW, GW)]).then_inc(gate_in, 16)
                if not isinstance(n, int) or n:
                    e.wait_ge(up_split, 2 * n)
                e.dma_start(up_raw, up_v[:, :, bass.ds(g * GW, GW)]).then_inc(up_in, 16)

            def load_down(n, g):
                e.wait_ge(gate_split, 2 * n + 2)
                e.dma_start(down_raw, down_v[bass.ds(g, 1), :, :, :].rearrange("g p f n -> (g p) f n")).then_inc(down_in, 16)

            def load_h2T(b, h):
                for c, dst in enumerate((h2T_hi[h], h2T_lo[h])):
                    e.dma_start(dst[:, :, :].bitcast(F32), h2_d[:, c, :, b * BLK + h * 512:b * BLK + (h + 1) * 512])\
                        .then_inc(h2T_in[h], 16)

            tile2(0, 0, 0, 0, True)
            tile2(0, 1, 1, 0, True)
            load_gate_up(0, 0)
            with e.Fori(1, TILES // 2 - 1) as j:
                for par in range(2):
                    tile2(j, par, 2, 0, True)
            e.wait_ge(h2_out, 32 * (TILES - 3))
            load_h2T(0, 0)
            tile2(TILES // 2 - 1, 0, 2, 0, False)
            tile2(TILES // 2 - 1, 1, 2, 1, False)
            e.wait_ge(mm2_full, TILES)
            e.wait_ge(h2n_done, TILES)
            for p in range(2):
                e.wait_ge(x1_out[p], 16 * (TILES // 2))
            load_h2T(0, 1)
            load_down(0, 0)
            e.dma_start(postf[:, :], post_ffn).then_inc(post_in, 16)
            h2_store(TILES - 1, h2s_end)

            load_gate_up(1, 1)
            for b in range(NB):
                with e.Fori(1 if b == 0 else 0, NG - 1) as g:
                    load_down(b * NG + g, g)
                    load_gate_up(b * NG + g + 1, g + 1)
                n = b * NG + NG - 1
                load_down(n, NG - 1)
                if b + 1 < NB:
                    load_gate_up(n + 1, 0)
                    if b == 0:
                        e.wait_ge(h2_out, 32 * TILES)
                    e.wait_ge(gu_full[1], 2 * n + 1)
                    load_h2T(b + 1, 0)
                    e.wait_ge(gu_full[1], 2 * n + 2)
                    load_h2T(b + 1, 1)
                for t in range(BT + 2):
                    if t >= 2:
                        s = b * BT + t - 2
                        e.wait_ge(out_done, s + 1)
                        e.dma_start(out[rows(s), :], x1r[s % 2][:, :]).then_inc(out_stored[s % 2], 16)
                    if t < BT:
                        s = b * BT + t
                        if s >= 2:
                            e.wait_ge(out_stored[s % 2], 16 * (s // 2))
                        e.dma_start(x1r[s % 2][:, :], x1_d[rows(s), :]).then_inc(x1r_in[s % 2], 16)
            for p in range(2):
                e.wait_ge(out_stored[p], 16 * (TILES // 2))

        @block.gpsimd
        def _(e):
            e.memset(ident[:, :], 0.0).then_inc(id_zero, 1)
            e.memset(mhalf[:, :], -0.5).then_inc(pool_consts, 1)
            e.memset(pbias[:, :], NEG).then_inc(pool_consts, 1)
            e.memset(kA[0][:, :], 0.0).then_inc(pool_consts, 1)
            e.memset(vA[0][:, :], 0.0).then_inc(pool_consts, 1)
            e.wait_ge(id_zero, 1)
            e.affine_select(out=ident[:, :], in_=ident[:, :], compare_op=ALU.not_equal, fill=1.0,
                            base=0, pattern=[[-1, P]], channel_multiplier=1).then_inc(pool_consts, 1)
            e.wait_ge(pool_consts, 5)

            def rstd_x(m, par):
                e.wait_ge(msx_ready, m + 1)
                e.tensor_tensor(rstdx[:, par:par + 1], msx[:, par:par + 1], mhalf[:, 0:1],
                                ALU.pow).then_inc(rstdx_ready, 1)

            def tile(j, par, before, last, ahead):
                k = 2 * j + par
                e.wait_ge(rope_mul, 3 * k + 3)
                if before:
                    e.wait_ge(t_full[0], 3 * k)
                    e.wait_ge(t_full[1], 3 * k)
                qv = "p (kv i d) -> p kv i d"
                e.tensor_tensor(qrot[:, :].rearrange("p (i kv d) -> p kv i d", kv=KVH, d=HD),
                                ropeA[:, 0:AW].rearrange(qv, kv=KVH, d=HD),
                                ropeB[:, 0:AW].rearrange(qv, kv=KVH, d=HD), ALU.add).then_inc(rot_done, 1)
                e.tensor_tensor(krot[:, :], ropeA[:, AW:AW + P], ropeB[:, AW:AW + P],
                                ALU.add).then_inc(rot_done, 1)
                if ahead:
                    rstd_x(k + 2, par)
                e.wait_ge(var_ready, k + 1)
                e.tensor_tensor(rstdv[:, :], varm[:, :], mhalf[:, 0:1], ALU.pow).then_inc(rstdv_ready, 1)
                e.wait_ge(vhat_done, k + 1)
                e.tensor_tensor(vn1[:, :], vhat[:, :], lng[:, :], ALU.mult).then_inc(vn1_done, 1)
                if before:
                    e.wait_ge(g_full, k)
                e.wait_ge(vn1_done, k + 1)
                e.tensor_tensor(vn[:, :], vn1[:, :], lnb[:, :], ALU.add).then_inc(vn_ready, 1)
                e.wait_ge(ms2_ready, k + 1)
                e.tensor_tensor(rs2[:, :], ms2[:, :], mhalf[:, 0:2], ALU.pow).then_inc(rs2_ready, 1)

            rstd_x(0, 0)
            rstd_x(1, 1)
            e.wait_ge(consts, 16 * 7)
            e.memset(sgu_w[CH:P, :, 0:CH], 0.0).then_inc(pool_consts, 1)
            e.wait_ge(pool_consts, 6)
            over_tiles(e, tile)

            def tile2(j, par, before, last, ahead):
                k = 2 * j + par
                e.wait_ge(msm_ready, k + 1)
                e.tensor_tensor(rstdm[:, par:par + 1], msm[:, par:par + 1], mhalf[:, 0:1],
                                ALU.pow).then_inc(rstdm_ready, 1)
                e.wait_ge(msy_ready, k + 1)
                e.tensor_tensor(rstdy[:, par:par + 1], msy[:, par:par + 1], mhalf[:, 0:1],
                                ALU.pow).then_inc(rstdy_ready, 1)

            over_tiles(e, tile2)

            for b in range(NB):
                e.wait_ge(mm2_full, TILES)
                if b == 0:
                    e.wait_ge(h2_out, 32 * TILES)
                else:
                    e.wait_ge(out_done, b * BT)
                e.memset(acc[:, :, :], 0.0).then_inc(acc_zero, 1)
                for t in range(BT):
                    s = b * BT + t
                    e.wait_ge(msf_ready, s + 1)
                    e.tensor_tensor(rstdf[:, t:t + 1], msf[:, t:t + 1], mhalf[:, 0:1], ALU.pow).then_inc(rstdf_ready, 1)
                    if t:
                        add_x1(e, s - 1)
                add_x1(e, b * BT + BT - 1)

        @block.scalar
        def _(e):
            def stats_x(m, j, par):
                e.wait_ge(x_in[par], 16 * (j + 1))
                e.activation(squares1[:, :], xt[par][:, :], ACT.Square,
                             accum_out=ssx[:, par:par + 1]).then_inc(ssx_done, 1)
                e.wait_ge(ssx_done, m + 1)
                e.activation(msx[:, par:par + 1], ssx[:, par:par + 1], ACT.Copy, scale=1.0 / D,
                             bias=EPS).then_inc(msx_ready, 1)

            def h_hi(par, use):
                for i in range(2):
                    e.wait_ge(t_full[i], use + 1)
                    e.activation(hT_hi[par][:, i * 512:(i + 1) * 512], T[i][:, :], ACT.Copy).then_inc(h_hi_done, 1)

            def tile(j, par, before, last, ahead):
                k = 2 * j + par
                if not last:
                    h_hi(1 - par, use_h(k))
                e.wait_ge(rope_mul, 3 * k + 3)
                if before:
                    e.wait_ge(pv_done, k)
                e.activation(vB[:, :], ZA[:, 1, P:2 * P], ACT.Copy).then_inc(v_done, 1)
                e.activation(vA[par][0:CH, :], ZA[0:CH, 1, P:2 * P], ACT.Copy).then_inc(v_done, 1)
                e.activation(vA[1 - par][CH:P, :], ZA[CH:P, 1, P:2 * P], ACT.Copy).then_inc(v_done, 1)
                if ahead:
                    stats_x(k + 2, j + 1, par)
                e.wait_ge(t_full[0], use_q(k, last) + 1)
                e.activation(qT[:, :], T0[:, :], ACT.Copy).then_inc(t_drained[0], 1)
                e.wait_ge(zus_full, k + 1)
                if before:
                    e.wait_ge(sB_done, k)
                e.activation(gel[:, :], flat(ZB[:, :, :]), ACT.Gelu).then_inc(gel_done, 1)
                e.wait_ge(soft_ready, 2 * k + 2)
                e.activation(esink[:, :], dsink[:, :], ACT.Exp).then_inc(exp_done, 1)
                for h in range(NH):
                    e.activation(probs[:, chunk(h)], S[:, h // PAIRS, chunk(h % PAIRS)],
                                 ACT.Exp, bias=mneg[:, h:h + 1], scale=HD ** -0.5,
                                 accum_out=den[:, h:h + 1]).then_inc(exp_done, 1)
                e.wait_ge(t_full[0], use_p(k, last) + 1)
                e.activation(probsT[:, 0:512], T0[:, :], ACT.Copy).then_inc(t_drained[0], 1)
                if last:
                    wout_hi_parts()
                    mix_hi(0, 0)
                e.wait_ge(sB_done, k + 1)
                e.activation(squares1[:, AW:D], sB[:, :], ACT.Square, accum_out=ss2[:, 1:2]).then_inc(ss2_done, 1)
                e.wait_ge(aO_done, k + 1)
                e.activation(squares1[:, 0:AW], aO[:, :], ACT.Square, accum_out=ss2[:, 0:1]).then_inc(ss2_done, 1)
                e.wait_ge(ss2_done, 2 * k + 2)
                e.activation(ms2[:, :], ss2[:, :], ACT.Copy, scale=1.0 / SW, bias=EPS).then_inc(ms2_ready, 1)

            def wout_hi_parts():
                e.wait_ge(zus_full, TILES)
                for c in range(KD):
                    e.wait_ge(wout_in[c], 16)
                    e.activation(wout_hi[:, c, :], wout_raw[c][:, :], ACT.Copy,
                                 scale=gcol_out[:, c:c + 1]).then_inc(wout_hi_done, 1)

            def mix_hi(k, par):
                for i in range(2):
                    e.wait_ge(mixT_full, 2 * k + i + 1)
                    e.activation(mixT_hi[par][:, i * 512:(i + 1) * 512], T[i][:, :], ACT.Copy).then_inc(mixT_hi_done, 1)

            stats_x(0, 0, 0)
            e.wait_ge(gains_in, 16)
            for i in range(len(PIECES)):
                c, w, raw = piece(i)
                e.wait_ge(wraw_in[i % 3], 16 * (i // 3 + 1))
                e.activation(win_hi[:, c, w], raw, ACT.Copy, scale=gcol_in[:, c:c + 1]).then_inc(win_hi_done, 1)
                if i == 1:
                    h_hi(0, 0)
                    stats_x(1, 0, 1)
            e.wait_ge(pool_consts, 6)
            e.wait_ge(consts, 16 * 7)
            over_tiles(e, tile)

            def h2_hi(k, first, dst=h2s):
                if not first:
                    e.wait_ge(h2_out, 32 * k)
                for i in range(2):
                    e.wait_ge(h2T_full, 2 * k + i + 1)
                    e.activation(flat(dst[:, 0, 4 * i:4 * i + 4, :]), S[:, i, :], ACT.Copy).then_inc(h2s_hi_done, 1)

            def tile2(j, par, before, last, ahead):
                k = 2 * j + par
                if not last:
                    mix_hi(k + 1, 1 - par)
                e.wait_ge(mm2_full, k + 1)
                e.activation(squares2[:, :], flat(M[par][:, :, :]), ACT.Square,
                             accum_out=ssm[:, par:par + 1]).then_inc(ssm_done, 1)
                e.wait_ge(ssm_done, k + 1)
                e.activation(msm[:, par:par + 1], ssm[:, par:par + 1], ACT.Copy, scale=1.0 / D,
                             bias=EPS).then_inc(msm_ready, 1)
                if before:
                    h2_hi(k - 1, before == 1)
                e.wait_ge(x1_done, k + 1)
                e.activation(squares2[:, :], xres[par][:, :], ACT.Square,
                             accum_out=ssy[:, par:par + 1]).then_inc(ssy_done, 1)
                e.wait_ge(ssy_done, k + 1)
                e.activation(msy[:, par:par + 1], ssy[:, par:par + 1], ACT.Copy, scale=1.0 / D,
                             bias=EPS).then_inc(msy_ready, 1)

            def gate_up_hi(n, f):
                if not isinstance(n, int) or n:
                    e.wait_ge(gu_full[f], 2 * n)
                e.wait_ge(gate_in, 16 * n + 16)
                e.activation(gu_hi[f][:, 0], gate_raw[:, :, chunk(f)], ACT.Copy).then_inc(gu_hi_done, 1)
                e.wait_ge(up_in, 16 * n + 16)
                e.activation(gu_hi[f][:, 1], up_raw[:, :, chunk(f)], ACT.Copy).then_inc(gu_hi_done, 1)

            tile2(0, 0, 0, 0, True)
            tile2(0, 1, 1, 0, True)
            with e.Fori(1, TILES // 2 - 1) as j:
                for par in range(2):
                    tile2(j, par, 2, 0, True)
            gate_up_hi(0, 0)
            tile2(TILES // 2 - 1, 0, 2, 0, False)
            gate_up_hi(0, 1)
            tile2(TILES // 2 - 1, 1, 2, 1, False)

            def unit(n, q):
                h, f = q // 2, q % 2
                e.wait_ge(gu_full[f], 2 * n + h + 1)
                e.activation(th[f][:, :], GU[f][:, 0, :], ACT.Tanh, scale=0.5).then_inc(th_done, 1)
                e.wait_ge(gu_drained[f], 2 * n + h + 1)
                if q == 0 and (not isinstance(n, int) or n):
                    e.wait_ge(dn_full[3], 4 * n)
                e.activation(act_hi[:, f, h * 512:(h + 1) * 512], prod[f][:, :], ACT.Copy,
                             scale=0.5).then_inc(act_hi_done, 1)

            def down_hi(n):
                if not isinstance(n, int) or n:
                    e.wait_ge(dn_full[3], 4 * n)
                e.wait_ge(down_in, 16 * n + 16)
                e.activation(flat(wd_hi[:, :, :]), raw_a[:, :], ACT.Copy).then_inc(wd_hi_done, 1)

            def group(n, more=True):
                unit(n, 0)
                if isinstance(n, int) and n == 0:
                    h2_hi(TILES - 1, True, h2s_end)
                unit(n, 1)
                down_hi(n)
                unit(n, 2)
                if more:
                    gate_up_hi(n + 1, 0)
                unit(n, 3)
                if more:
                    gate_up_hi(n + 1, 1)

            group(0)
            for b in range(NB):
                with e.Fori(1 if b == 0 else 0, NG - 1) as g:
                    group(b * NG + g)
                n = b * NG + NG - 1
                group(n, b + 1 < NB)
                for t in range(BT):
                    s = b * BT + t
                    for i in range(2):
                        e.wait_ge(acc_added[(2 * t + i) % 4], 4 * n + (2 * t + i) // 4 + 1)
                    e.activation(squares3[:, :], acc[:, t, :], ACT.Square, accum_out=ssf[:, t:t + 1]).then_inc(ssf_done, 1)
                    e.wait_ge(ssf_done, s + 1)
                    e.activation(msf[:, t:t + 1], ssf[:, t:t + 1], ACT.Copy, scale=1.0 / D, bias=EPS).then_inc(msf_ready, 1)

        @block.vector
        def _(e):
            def norm_x(m, par):
                e.wait_ge(rstdx_ready, m + 1)
                if not isinstance(m, int) or m:
                    e.wait_ge(t_full[1], 1 if isinstance(m, int) and m == 1 else 3 * m - 4)
                e.tensor_scalar(xn[:, :], xt[par][:, :], rstdx[:, par:par + 1], None,
                                ALU.mult).then_inc(xn_done, 1)

            def h_lo(par, m):
                for i in range(2):
                    e.wait_ge(h_hi_done, 2 * m + i + 1)
                    half = slice(i * 512, (i + 1) * 512)
                    e.tensor_tensor(hT_lo[par][:, half], T[i][:, :], hT_hi[par][:, half].bitcast(F32),
                                    ALU.subtract).then_inc(t_drained[i], 1)

            def tile(j, par, before, last, ahead):
                k = 2 * j + par
                e.wait_ge(zqkv_full, k + 1)
                if before:
                    e.wait_ge(rot_done, 2 * k)
                z = flat(ZA[:, :, :])[:, 0:AW + P]
                c = cs[:, bass.ds(k, 1), :]
                e.tensor_tensor(ropeA[:, :].rearrange("p (h d) -> p h d", d=32), z.rearrange("p (h d) -> p h d", d=32),
                                c[:, :, 0:32].to_broadcast([P, 20, 32]), ALU.mult).then_inc(rope_mul, 1)
                zz = z.rearrange("p (h t d) -> p h t d", t=2, d=32)
                rb = ropeB[:, :].rearrange("p (h t d) -> p h t d", t=2, d=32)
                for a in range(2):
                    e.tensor_tensor(rb[:, :, a, :], zz[:, :, 1 - a, :],
                                    c[:, :, 32 + 32 * a:64 + 32 * a].to_broadcast([P, 10, 32]),
                                    ALU.mult).then_inc(rope_mul, 1)
                if not last:
                    h_lo(1 - par, k + 1)
                e.wait_ge(t_full[1], use_q(k, last) + 1)
                e.tensor_copy(kB[:, :], T1[:, 0:P]).then_inc(k_done, 1)
                e.tensor_copy(kA[par][:, 0:CH], T1[:, 0:CH]).then_inc(k_done, 1)
                e.tensor_copy(kA[1 - par][:, CH:P], T1[:, CH:P]).then_inc(t_drained[1], 1)
                e.wait_ge(s_full, k + 1)
                first_q = S[0:CH, :, :].rearrange("p a (h n) -> p (a h) n", n=P)[:, :, CH:P]
                if not before:
                    e.tensor_scalar(first_q, first_q, pbias[0:CH, 0:1], None, ALU.add).then_inc(masked, 1)
                    e.wait_ge(masked, 1)
                e.tensor_reduce(mraw[:, :], S[:, :, :].rearrange("p a (h n) -> p (a h) n", n=P), AX_X,
                                ALU.max).then_inc(mraw_done, 1)
                e.wait_ge(mraw_done, k + 1)
                e.scalar_tensor_tensor(out=mtop[:, :], in0=mraw[:, :], scalar=HD ** -0.5, in1=sinkb[:, :],
                                       op0=ALU.mult, op1=ALU.max).then_inc(mtop_done, 1)
                e.wait_ge(mtop_done, k + 1)
                e.tensor_scalar(mneg[:, :], mtop[:, :], -1.0, None, ALU.mult).then_inc(soft_ready, 1)
                e.tensor_tensor(dsink[:, :], sinkb[:, :], mtop[:, :], ALU.subtract).then_inc(soft_ready, 1)
                e.wait_ge(gel_done, k + 1)
                e.bn_stats(st6[:, :], gel[:, SW:2 * SW]).then_inc(st6_done, 1)
                if ahead:
                    norm_x(k + 2, par)
                e.wait_ge(st6_done, k + 1)
                passed(e, passed_dve)
                e.bn_aggr(mv[:, :], st6[:, :]).then_inc(mv_done, 1)
                e.wait_ge(mv_done, k + 1)
                e.tensor_scalar(varm[:, :], mv[:, 1:2], EPS, None, ALU.add).then_inc(var_ready, 1)
                e.wait_ge(rstdv_ready, k + 1)
                e.tensor_scalar(vhat[:, :], gel[:, SW:2 * SW], mv[:, 0:1], rstdv[:, 0:1], ALU.subtract,
                                ALU.mult).then_inc(vhat_done, 1)
                e.wait_ge(exp_done, 9 * k + 9)
                e.tensor_tensor(dtot[:, :], den[:, :], esink[:, :], ALU.add).then_inc(dtot_done, 1)
                e.wait_ge(dtot_done, k + 1)
                e.reciprocal(rden[:, :], dtot[:, :]).then_inc(rden_done, 1)
                e.wait_ge(t_full[1], use_p(k, last) + 1)
                e.tensor_copy(probsT[:, 512:1024], T1[:, :]).then_inc(t_drained[1], 1)
                if last:
                    wout_lo_parts()
                    mix_lo(0, 0)
                e.wait_ge(g_full, k + 1)
                for g in range(SG):
                    ins = e.scalar_tensor_tensor(out=sB[:, chunk(g)], in0=S[:, 1, chunk(g)], scalar=sgub[:, g:g + 1],
                                                 in1=gel[:, chunk(g)], op0=ALU.add, op1=ALU.mult)
                ins.then_inc(sB_done, 1)
                e.wait_ge(pv_done, k + 1)
                e.wait_ge(rden_done, k + 1)
                e.tensor_tensor(aO[:, :].rearrange("p (h d) -> p h d", d=HD),
                                S[:, 0, :].rearrange("p (h d) -> p h d", d=HD),
                                rden[:, :].unsqueeze(2).to_broadcast([P, NH, HD]), ALU.mult).then_inc(aO_done, 1)
                if before == 2:
                    e.wait_ge(mix_out[par], 16 * j)
                e.wait_ge(rs2_ready, k + 1)
                e.tensor_scalar(mix[par][:, AW:D], sB[:, :], rs2[:, 1:2], None, ALU.mult).then_inc(mix_done, 1)
                e.tensor_scalar(mix[par][:, 0:AW], aO[:, :], rs2[:, 0:1], None, ALU.mult).then_inc(mix_done, 1)

            def wout_lo_parts():
                for c in range(KD):
                    e.wait_ge(wout_hi_done, c + 1)
                    e.scalar_tensor_tensor(out=wout_lo[:, c, :], in0=wout_raw[c][:, :], scalar=gcol_out[:, c:c + 1],
                                           in1=wout_hi[:, c, :].bitcast(F32), op0=ALU.mult,
                                           op1=ALU.subtract).then_inc(wout_split, 1)

            def mix_lo(k, par):
                for i in range(2):
                    e.wait_ge(mixT_hi_done, 2 * k + i + 1)
                    half = slice(i * 512, (i + 1) * 512)
                    e.tensor_tensor(mixT_lo[par][:, half], T[i][:, :], mixT_hi[par][:, half].bitcast(F32),
                                    ALU.subtract).then_inc(mixT_split, 1)

            norm_x(0, 0)
            e.wait_ge(gains_in, 16)
            for i in range(len(PIECES)):
                c, w, raw = piece(i)
                e.wait_ge(win_hi_done, i + 1)
                e.scalar_tensor_tensor(out=win_lo[:, c, w], in0=raw, scalar=gcol_in[:, c:c + 1],
                                       in1=win_hi[:, c, w].bitcast(F32), op0=ALU.mult,
                                       op1=ALU.subtract).then_inc(win_split, 1)
                if i == 1:
                    h_lo(0, 0)
                    norm_x(1, 1)
            e.wait_ge(pool_consts, 6)
            e.wait_ge(consts, 16 * 7)
            over_tiles(e, tile)

            e.wait_ge(posts, 32)

            def h2_lo(k, dst=h2s):
                for i in range(2):
                    e.wait_ge(h2s_hi_done, 2 * k + i + 1)
                    ks = slice(4 * i, 4 * i + 4)
                    e.tensor_tensor(flat(dst[:, 1, ks, :]), S[:, i, :], flat(dst[:, 0, ks, :]).bitcast(F32),
                                    ALU.subtract).then_inc(h2s_split, 1)

            def tile2(j, par, before, last, ahead):
                k = 2 * j + par
                if not last:
                    mix_lo(k + 1, 1 - par)
                e.wait_ge(rstdm_ready, k + 1)
                e.scalar_tensor_tensor(out=ytmp[:, :], in0=flat(M[par][:, :, :]), scalar=rstdm[:, par:par + 1],
                                       in1=postm[:, :], op0=ALU.mult, op1=ALU.mult).then_inc(y_done, 1)
                e.wait_ge(xres_in[par], 16 * (j + 1))
                e.wait_ge(y_done, k + 1)
                e.tensor_tensor(xres[par][:, :], ytmp[:, :], xres[par][:, :], ALU.add).then_inc(x1_done, 1)
                if before:
                    h2_lo(k - 1)
                    e.wait_ge(h2T_full, 2 * k)
                e.wait_ge(rstdy_ready, k + 1)
                e.scalar_tensor_tensor(out=h2n[:, :], in0=xres[par][:, :], scalar=rstdy[:, par:par + 1],
                                       in1=pref[:, :], op0=ALU.mult, op1=ALU.mult).then_inc(h2n_done, 1)

            def gate_up_lo(n, f):
                for c, (raw, done) in enumerate(((gate_raw, gate_split), (up_raw, up_split))):
                    e.wait_ge(gu_hi_done, 4 * n + 2 * f + c + 1)
                    e.tensor_tensor(gu_lo[f][:, c], raw[:, :, chunk(f)], gu_hi[f][:, c].bitcast(F32),
                                    ALU.subtract).then_inc(done, 1)

            tile2(0, 0, 0, 0, True)
            tile2(0, 1, 1, 0, True)
            with e.Fori(1, TILES // 2 - 1) as j:
                for par in range(2):
                    tile2(j, par, 2, 0, True)
            gate_up_lo(0, 0)
            tile2(TILES // 2 - 1, 0, 2, 0, False)
            gate_up_lo(0, 1)
            tile2(TILES // 2 - 1, 1, 2, 1, False)

            def unit(n, q):
                h, f = q // 2, q % 2
                e.wait_ge(th_done, 4 * n + q + 1)
                e.scalar_tensor_tensor(out=sil[f][:, :], in0=th[f][:, :], scalar=1.0, in1=GU[f][:, 0, :],
                                       op0=ALU.add, op1=ALU.mult).then_inc(sil_done, 1)
                e.wait_ge(sil_done, 4 * n + q + 1)
                e.tensor_tensor(prod[f][:, :], sil[f][:, :], GU[f][:, 1, :], ALU.mult).then_inc(gu_drained[f], 1)
                e.wait_ge(act_hi_done, 4 * n + q + 1)
                half = slice(h * 512, (h + 1) * 512)
                e.scalar_tensor_tensor(out=act_lo[:, f, half], in0=prod[f][:, :], scalar=0.5,
                                       in1=act_hi[:, f, half].bitcast(F32), op0=ALU.mult,
                                       op1=ALU.subtract).then_inc(act_split, 1)

            def down_lo(n):
                e.wait_ge(wd_hi_done, n + 1)
                e.tensor_tensor(flat(wd_lo[:, :, :]), raw_a[:, :], flat(wd_hi[:, :, :]).bitcast(F32),
                                ALU.subtract).then_inc(wd_split, 1)

            def scale_out(b, t):
                e.wait_ge(rstdf_ready, b * BT + t + 1)
                e.scalar_tensor_tensor(out=acc[:, t, :], in0=acc[:, t, :], scalar=rstdf[:, t:t + 1],
                                       in1=postf[:, :], op0=ALU.mult, op1=ALU.mult).then_inc(yf_done, 1)

            def group(n, b, end=False, more=True):
                unit(n, 0)
                if isinstance(n, int) and n == 0:
                    h2_lo(TILES - 1, h2s_end)
                unit(n, 1)
                down_lo(n)
                unit(n, 2)
                if more:
                    gate_up_lo(n + 1, 0)
                unit(n, 3)
                e.wait_ge(acc_zero, b + 1)
                for i in range(2 * BT):
                    t, d = i // 2, i % 2
                    e.wait_ge(dn_full[i % 4], 4 * n + i // 4 + 1)
                    a = acc[:, t, d * 512:(d + 1) * 512]
                    e.tensor_tensor(a, DN[i % 4], a, ALU.add).then_inc(acc_added[i % 4], 1)
                    if end and t and d:
                        scale_out(b, t - 1)
                if end:
                    scale_out(b, BT - 1)
                if more:
                    gate_up_lo(n + 1, 1)

            e.wait_ge(post_in, 16)
            e.wait_ge(h2_out, 32 * (TILES - 1))
            group(0, 0)
            for b in range(NB):
                with e.Fori(1 if b == 0 else 0, NG - 1) as g:
                    group(b * NG + g, b)
                group(b * NG + NG - 1, b, end=True, more=b + 1 < NB)

        @block.tensor
        def _(e):
            def three(out_ap, lhi, llo, rhi, rlo, start, stop):
                e.matmul(out_ap, lhi, rhi, start=start, stop=False)
                e.matmul(out_ap, lhi, rlo, start=False, stop=False)
                return e.matmul(out_ap, llo, rhi, start=False, stop=stop)

            def h_transposes(m, use):
                e.wait_ge(xn_done, m + 1)
                for i in range(2):
                    if not isinstance(use, int) or use:
                        e.wait_ge(t_drained[i], use)
                    for c in range(4):
                        ins = e.transpose(T[i][:, chunk(c)], xn[:, chunk(4 * i + c)], ident[:, :])
                    ins.then_inc(t_full[i], 1)

            def z_columns(out_ap, par, w):
                for c in range(KD):
                    ins = three(out_ap, hT_hi[par][:, chunk(c)], hT_lo[par][:, chunk(c)], win_hi[:, c, w],
                                win_lo[:, c, w], c == 0, c == KD - 1)
                return ins

            def z_qkv(m, par, use, first=False):
                for i in range(2):
                    e.wait_ge(t_drained[i], use + 1)
                if not first:
                    e.wait_ge(rope_mul, 3 * m)
                    e.wait_ge(v_done, 3 * m)
                z_columns(ZA[:, 0, :], par, slice(0, AW))
                z_columns(ZA[:, 1, 0:2 * P], par, slice(AW, AW + 2 * P)).then_inc(zqkv_full, 1)

            def tile(j, par, before, last, ahead):
                k = 2 * j + par
                if not last:
                    h_transposes(k + 1, use_h(k))
                if before:
                    e.wait_ge(gel_done, k)
                else:
                    e.wait_ge(win_split, 2 * KD)
                z_columns(ZB[:, 0, :], par, slice(768, 768 + SW)).then_inc(zu_full, 1)
                e.wait_ge(rot_done, 2 * k + 2)
                e.wait_ge(t_drained[0], use_q(k, last))
                for i in range(PAIRS):
                    ins = e.transpose(T0[:, chunk(i)], qrot[:, chunk(i)], ident[:, :])
                ins.then_inc(t_full[0], 1)
                e.wait_ge(t_drained[1], use_q(k, last))
                e.transpose(T1[:, 0:P], krot[:, :], ident[:, :]).then_inc(t_full[1], 1)
                z_columns(ZB[:, 1, :], par, slice(768 + SW, WIN)).then_inc(zus_full, 1)
                e.wait_ge(t_drained[0], use_q(k, last) + 1)
                e.wait_ge(t_drained[1], use_q(k, last) + 1)
                if before:
                    e.wait_ge(aO_done, k)
                    e.wait_ge(sB_done, k)
                passed(e, passed_pe)
                for i in range(PAIRS):
                    for half, keys in enumerate((kA[par], kB)):
                        for kv in range(KVH):
                            r = slice(kv * HD, (kv + 1) * HD)
                            ins = e.matmul(S[half * CH:(half + 1) * CH, kv, chunk(i)],
                                           qT[r, i * P + half * CH:i * P + (half + 1) * CH], keys[r, :],
                                           start=True, stop=True)
                ins.then_inc(s_full, 1)
                if not last:
                    z_qkv(k + 1, 1 - par, use_h(k))
                e.wait_ge(exp_done, 9 * k + 9)
                for i in range(2):
                    e.wait_ge(t_drained[i], use_p(k, last))
                    for c in range(4):
                        ins = e.transpose(T[i][:, chunk(c)], probs[:, chunk(4 * i + c)], ident[:, :])
                    ins.then_inc(t_full[i], 1)
                e.wait_ge(vn_ready, k + 1)
                for g in range(SG):
                    ins = e.matmul(S[:, 1, chunk(g)], sgu_w[:, g, :], vn[:, chunk(g)], start=True, stop=True)
                ins.then_inc(g_full, 1)
                e.wait_ge(t_drained[0], use_p(k, last) + 1)
                e.wait_ge(t_drained[1], use_p(k, last) + 1)
                e.wait_ge(v_done, 3 * k + 3)
                for h in range(NH):
                    kv = h // PAIRS
                    for half, vals in enumerate((vA[par], vB)):
                        ins = e.matmul(S[half * CH:(half + 1) * CH, 0, h * HD:(h + 1) * HD],
                                       probsT[:, h * P + half * CH:h * P + (half + 1) * CH],
                                       vals[:, kv * HD:(kv + 1) * HD], start=True, stop=True)
                ins.then_inc(pv_done, 1)

            e.wait_ge(pool_consts, 5)
            h_transposes(0, 0)
            e.wait_ge(win_split, KD)
            z_qkv(0, 0, 0, first=True)
            e.wait_ge(pool_consts, 6)
            over_tiles(e, tile)

            def mix_transposes(k, j, par):
                e.wait_ge(mix_in[par], 16 * (j + 1))
                if not isinstance(k, int) or k:
                    e.wait_ge(mixT_split, 2 * k)
                for i in range(2):
                    for c in range(4):
                        ins = e.transpose(T[i][:, chunk(c)], mixin[par][:, chunk(4 * i + c)], ident[:, :])
                    ins.then_inc(mixT_full, 1)

            def h2_transposes(k, first=False):
                e.wait_ge(h2n_done, k + 1)
                if not first:
                    e.wait_ge(h2s_split, 2 * k)
                for i in range(2):
                    for c in range(4):
                        ins = e.transpose(S[:, i, chunk(c)], h2n[:, chunk(4 * i + c)], ident[:, :])
                    ins.then_inc(h2T_full, 1)

            def tile2(j, par, before, last, ahead):
                k = 2 * j + par
                if not last:
                    mix_transposes(k + 1, j + par, 1 - par)
                e.wait_ge(mixT_split, 2 * k + 2)
                if before == 2:
                    e.wait_ge(y_done, k - 1)
                for a in range(2):
                    for c in range(KD):
                        w = slice(a * 512, (a + 1) * 512)
                        ins = three(M[par][:, a, :], mixT_hi[par][:, chunk(c)], mixT_lo[par][:, chunk(c)],
                                    wout_hi[:, c, w], wout_lo[:, c, w], c == 0, c == KD - 1)
                ins.then_inc(mm2_full, 1)
                if before:
                    if before == 1:
                        e.wait_ge(aO_done, TILES)
                    h2_transposes(k - 1, before == 1)

            mix_transposes(0, 0, 0)
            e.wait_ge(wout_split, KD)
            over_tiles(e, tile2)

            def group(n, b):
                for q in range(4):
                    h, f = q // 2, q % 2
                    if h == 0:
                        e.wait_ge(gate_split, 2 * n + f + 1)
                        e.wait_ge(up_split, 2 * n + f + 1)
                    if not (isinstance(n, int) and n == 0 and h == 0):
                        e.wait_ge(gu_drained[f], 2 * n + h)
                    e.wait_ge(h2T_in[h], 32 * (b + 1))
                    for a in range(2):
                        for c in range(KD):
                            ins = three(GU[f][:, a, :], gu_hi[f][:, a, c, :], gu_lo[f][:, a, c, :],
                                        h2T_hi[h][:, c, :], h2T_lo[h][:, c, :], c == 0, c == KD - 1)
                    ins.then_inc(gu_full[f], 1)
                    if isinstance(n, int) and n == 0 and q == 0:
                        h2_transposes(TILES - 1)
                e.wait_ge(wd_split, n + 1)
                for i in range(2 * BT):
                    t, d = i // 2, i % 2
                    if i == 0:
                        e.wait_ge(act_split, 4 * n + 2)
                    if i == BT:
                        e.wait_ge(act_split, 4 * n + 4)
                    if not (isinstance(n, int) and n == 0 and i < 4):
                        e.wait_ge(acc_added[i % 4], 4 * n + i // 4)
                    for f in range(2):
                        w = slice(d * 512, (d + 1) * 512)
                        ins = three(DN[i % 4], act_hi[:, f, chunk(t)], act_lo[:, f, chunk(t)], wd_hi[:, f, w],
                                    wd_lo[:, f, w], f == 0, f == 1)
                    ins.then_inc(dn_full[i % 4], 1)

            e.wait_ge(y_done, TILES - 1)
            group(0, 0)
            for b in range(NB):
                with e.Fori(1 if b == 0 else 0, NG - 1) as g:
                    group(b * NG + g, b)
                group(b * NG + NG - 1, b)


def rope_table():
    inv = np.float32(1) / (10000.0 ** (np.arange(0, HD, 2) / HD)).astype(np.float32)
    ang = (np.arange(SEQ, dtype=np.float32)[:, None] * inv[None, :]).astype(np.float32).astype(np.float64)
    t = np.concatenate([np.cos(ang), -np.sin(ang), np.sin(ang)], axis=1).astype(np.float32)
    return np.ascontiguousarray(t.reshape(TILES, P, 96).transpose(1, 0, 2))


def kernel(x, norm_mix_pre, norm_mix_post, w_in, attn_sinks, sgu_ln_g, sgu_ln_b, sgu_w, sgu_b,
           norm_out_attn, norm_out_sgu, w_out, norm_ffn_pre, norm_ffn_post, w_gate, w_up, w_down):
    import concourse.bacc as bacc
    from concourse.bass_utils import run_bass_kernel_spmd

    def cols(*v):
        return np.concatenate([np.asarray(a)[0] for a in v]).reshape(KD, P).T

    def bcast(v):
        return np.broadcast_to(np.asarray(v)[0], (P, np.asarray(v).shape[1]))

    arrays = {
        "x": np.asarray(x)[0], "w_in": np.asarray(w_in)[0], "w_out": np.asarray(w_out)[0],
        "w_gate": np.asarray(w_gate)[0], "w_up": np.asarray(w_up)[0], "w_down": np.asarray(w_down)[0],
        "gain_in": cols(norm_mix_pre), "gain_out": cols(norm_out_attn, norm_out_sgu),
        "post_mix": bcast(norm_mix_post), "pre_ffn": bcast(norm_ffn_pre), "post_ffn": bcast(norm_ffn_post),
        "sinks": bcast(attn_sinks), "ln_g": bcast(sgu_ln_g), "ln_b": bcast(sgu_ln_b),
        "sgu_wt": np.asarray(sgu_w)[0].transpose(2, 0, 1), "sgu_bt": np.asarray(sgu_b)[0].T,
        "rope": rope_table(),
    }
    arrays = {n: np.ascontiguousarray(a) for n, a in arrays.items()}
    nc = bacc.Bacc("TRN2", target_bir_lowering=False, num_devices=1)
    args = {n: nc.dram_tensor(n, a.shape, mybir.dt.from_np(a.dtype), kind="ExternalInput").ap()
            for n, a in arrays.items()}
    out = nc.dram_tensor("out", (SEQ, D), F32, kind="ExternalOutput").ap()
    build_kernel(nc, out=out, **args)
    r = run_bass_kernel_spmd(nc, [arrays], core_ids=[0])
    return r.results[0]["out"].reshape(1, SEQ, D)
```

```python
import numpy as np

import concourse.bass as bass
from concourse import mybir

F32 = mybir.dt.float32
F32R = mybir.dt.float32r
BF16 = mybir.dt.bfloat16
ALU = mybir.AluOpType
ACT = mybir.ActivationFunctionType
AX_X = mybir.AxisListType.X

P = 128
SEQ, D = 2048, 1024
KD = D // P
TILES = SEQ // P
HD, NH, KVH = 64, 8, 2
PAIRS = NH // KVH
AW = NH * HD
SW = 512
SG = SW // P
CH = 64
QKV = AW + 2 * KVH * HD
WIN = QKV + 2 * SW
DFF = 2816
BLK = 1024
NB = SEQ // BLK
BT = BLK // P
GW = 256
NG = DFF // GW
RAWS = 6
ENDS = 2
EPS = 1e-6
NEG = -1e30


def build_kernel(nc, x, w_in, w_out, w_gate, w_up, w_down, gain_in, gain_out, post_mix, pre_ffn,
                 post_ffn, sinks, ln_g, ln_b, sgu_wt, sgu_bt, rope, out):
    mix_d = nc.dram_tensor("mix_d", (SEQ, D), F32).ap()
    x1_d = nc.dram_tensor("x1_d", (SEQ, D), F32).ap()
    h2_d = nc.dram_tensor("h2_d", (P, 2, KD, SEQ), F32).ap()

    KB = 1024
    START = 16512

    def at(name, kb, shape, dt=F32):
        return nc.alloc_sbuf_tensor_at(name, [P] + list(shape), dt, offset=START + int(kb * KB))

    wq_hi = at("wq_hi", 90, [KD, QKV], F32R)
    wq_lo = at("wq_lo", 114, [KD, QKV], F32R)
    wg_hi = at("wg_hi", 138, [KD, 2 * SW], F32R)
    wg_lo = at("wg_lo", 170, [KD, 2 * SW], F32R)
    wraw = [at(f"wraw{i}", 10 + 4 * i if i < 4 else 48 + 4 * i, [2 * SW]) for i in range(RAWS)]
    ropeA = at("ropeA", 0, [AW + P])
    ropeB = at("ropeB", 2.5, [AW + P])
    qT = at("qT", 5, [AW])
    kA = [at(f"kA{i}", 7 + 0.5 * i, [P]) for i in range(2)]
    kB = at("kB", 8, [P])
    vA = [at(f"vA{i}", 8.5 + 0.5 * i, [P]) for i in range(2)]
    vB = at("vB", 9.5, [P])
    probs = at("probs", 10, [NH * P])
    probsT = at("probsT", 14, [NH * P])
    gel = at("gel", 18, [2 * SW])
    vhat = at("vhat", 22, [SW])
    vn1 = at("vn1", 24, [SW])
    vn = at("vn", 26, [SW])
    sB = at("sB", 28, [SW])
    aO = at("aO", 30, [AW])
    hT_hi = [at(f"hT_hi{i}", 32 + 4 * i, [D], F32R) for i in range(2)]
    hT_lo = [at(f"hT_lo{i}", 40 + 4 * i, [D], F32R) for i in range(2)]
    xt = [at(f"xt{i}", 48 + 4 * i, [D]) for i in range(2)]
    xn = at("xn", 56, [D])
    qrot = at("qrot", 60, [AW])
    krot = at("krot", 62, [P])
    mix = [at(f"mix{i}", 64 + 4 * i, [D]) for i in range(2)]
    cs = at("cs", 72, [TILES, 96])
    lng = at("lng", 78, [SW])
    lnb = at("lnb", 80, [SW])
    squares1 = at("squares1", 82, [D], BF16)

    wout_raw = [at(f"wout_raw{c}", 88 + 4 * c, [D]) for c in range(KD)]
    wout_hi = at("wout_hi", 120, [KD, D], F32R)
    wout_lo = at("wout_lo", 152, [KD, D], F32R)
    mixT_hi = [at(f"mixT_hi{i}", 32 + 4 * i, [D], F32R) for i in range(2)]
    mixT_lo = [at(f"mixT_lo{i}", 40 + 4 * i, [D], F32R) for i in range(2)]
    mixin = [at(f"mixin{i}", 48 + 4 * i, [D]) for i in range(2)]
    xres = [at(f"xres{i}", 56 + 4 * i, [D]) for i in range(2)]
    ytmp = at("ytmp", 112, [D])
    h2s = at("h2s", 188, [2, KD, P], F32R)
    h2s_end = at("h2s_end", 168, [2, KD, P], F32R)
    postm = at("postm", 196, [D])
    pref = at("pref", 184, [D])
    h2n = at("h2n", 116, [D])
    squares2 = at("squares2", 200, [D], BF16)

    h2T_hi = [at(f"h2T_hi{h}", 32 * h, [KD, 512], F32R) for h in range(2)]
    h2T_lo = [at(f"h2T_lo{h}", 32 * h + 16, [KD, 512], F32R) for h in range(2)]
    gu_hi = [at(f"gu_hi{f}", 64 + 8 * f, [2, KD, P], F32R) for f in range(2)]
    gu_lo = [at(f"gu_lo{f}", 80 + 8 * f, [2, KD, P], F32R) for f in range(2)]
    raw_a = at("raw_a", 96, [KD * GW])
    raw_b = at("raw_b", 104, [KD * GW])
    act_hi = at("act_hi", 112, [2, BLK], F32R)
    act_lo = at("act_lo", 120, [2, BLK], F32R)
    wd_hi = at("wd_hi", 128, [2, D], F32R)
    wd_lo = at("wd_lo", 136, [2, D], F32R)
    acc = at("acc", 144, [BT, D])
    th = [at(f"th{i}", 176 + 2 * i, [512]) for i in range(2)]
    sil = [at(f"sil{i}", 180 + 2 * i, [512]) for i in range(2)]
    prod = [at(f"prod{i}", 184 + 2 * i, [512]) for i in range(2)]
    postf = at("postf", 188, [D])
    x1r = [at(f"x1r{i}", 192 + 4 * i, [D]) for i in range(2)]
    x1e = at("x1e", 0, [BT, D])
    squares3 = at("squares3", 200, [D], BF16)

    place = [202.0]

    def small(name, *shape):
        t = at(name, place[0], shape)
        place[0] += (4 * int(np.prod(shape)) + 31) // 32 * 32 / KB
        return t

    ident = small("ident", P)
    gcol_in, gcol_out = small("gcol_in", KD), small("gcol_out", KD)
    mhalf = small("mhalf", 2)
    sgu_w = small("sgu_w", SG, P)
    sgub, sinkb = small("sgub", SG), small("sinkb", NH)
    ssx, msx, rstdx = small("ssx", 2), small("msx", 2), small("rstdx", 2)
    pbias = small("pbias", 1)
    mraw, mtop, mneg, dsink = (small(n, NH) for n in ("mraw", "mtop", "mneg", "dsink"))
    den, esink, dtot, rden = (small(n, NH) for n in ("den", "esink", "dtot", "rden"))
    st6, mv, varm, rstdv = small("st6", 6), small("mv", 2), small("varm", 1), small("rstdv", 1)
    ss2, ms2, rs2 = small("ss2", 2), small("ms2", 2), small("rs2", 2)
    ssm, msm, rstdm = small("ssm", 2), small("msm", 2), small("rstdm", 2)
    ssy, msy, rstdy = small("ssy", 2), small("msy", 2), small("rstdy", 2)
    ssf, msf, rstdf = small("ssf", BT), small("msf", BT), small("rstdf", BT)
    assert START + place[0] * KB <= nc.sbuf_usable_end

    T0 = nc.alloc_psum_tensor("T0", [P, 512], F32)
    T1 = nc.alloc_psum_tensor("T1", [P, 512], F32)
    S = nc.alloc_psum_tensor("S", [P, 2, 512], F32)
    ZA = nc.alloc_psum_tensor("ZA", [P, 2, 512], F32)
    ZB = nc.alloc_psum_tensor("ZB", [P, 2, 512], F32)
    T = [T0, T1]
    M = [ZA, ZB]
    GU = [ZA, ZB]
    DN = [T0[:, :], T1[:, :], S[:, 0, :], S[:, 1, :]]

    sem = nc.alloc_semaphore

    def pair(name):
        return [sem(f"{name}{i}") for i in range(2)]

    gains_in, consts, posts, post_in = sem("gains_in"), sem("consts"), sem("posts"), sem("post_in")
    cs_in = sem("cs_in")
    wraw_in = [sem(f"wraw_in{i}") for i in range(RAWS)]
    win_hi_done, win_split = sem("win_hi_done"), sem("win_split")
    x_in, mix_out = pair("x_in"), pair("mix_out")
    id_zero, pool_consts = sem("id_zero"), sem("pool_consts")
    ssx_done, msx_ready, rstdx_ready, xn_done = sem("ssx_done"), sem("msx_ready"), sem("rstdx_ready"), sem("xn_done")
    t_full, t_drained = pair("t_full"), pair("t_drained")
    h_hi_done, zqkv_full, zus_full = sem("h_hi_done"), sem("zqkv_full"), sem("zus_full")
    rope_mul, rot_done, v_done, k_done = sem("rope_mul"), sem("rot_done"), sem("v_done"), sem("k_done")
    gel_done, st6_done, mv_done, var_ready = sem("gel_done"), sem("st6_done"), sem("mv_done"), sem("var_ready")
    rstdv_ready, vhat_done, vn1_done, vn_ready = sem("rstdv_ready"), sem("vhat_done"), sem("vn1_done"), sem("vn_ready")
    s_full, masked, mraw_done = sem("s_full"), sem("masked"), sem("mraw_done")
    mtop_done, soft_ready, exp_done = sem("mtop_done"), sem("soft_ready"), sem("exp_done")
    dtot_done, rden_done, g_full, pv_done = sem("dtot_done"), sem("rden_done"), sem("g_full"), sem("pv_done")
    sB_done, aO_done, ss2_done, ms2_ready = sem("sB_done"), sem("aO_done"), sem("ss2_done"), sem("ms2_ready")
    rs2_ready, mix_done = sem("rs2_ready"), sem("mix_done")
    wout_in = [sem(f"wout_in{c}") for c in range(KD)]
    wout_hi_done, wout_split = sem("wout_hi_done"), sem("wout_split")
    mix_in, xres_in, x1_out, h2_out = pair("mix_in"), pair("xres_in"), pair("x1_out"), sem("h2_out")
    mixT_full, mixT_hi_done, mixT_split, mm2_full = sem("mixT_full"), sem("mixT_hi_done"), sem("mixT_split"), sem("mm2_full")
    ssm_done, msm_ready, rstdm_ready = sem("ssm_done"), sem("msm_ready"), sem("rstdm_ready")
    y_done, x1_done, ssy_done, msy_ready = sem("y_done"), sem("x1_done"), sem("ssy_done"), sem("msy_ready")
    rstdy_ready, h2n_done, h2T_full = sem("rstdy_ready"), sem("h2n_done"), sem("h2T_full")
    h2s_hi_done, h2s_split = sem("h2s_hi_done"), sem("h2s_split")
    h2T_in = pair("h2T_in")
    gate_in, up_in, down_in = sem("gate_in"), sem("up_in"), sem("down_in")
    gu_hi_done, gate_split, up_split = sem("gu_hi_done"), sem("gate_split"), sem("up_split")
    wd_hi_done, wd_split = sem("wd_hi_done"), sem("wd_split")
    gu_full, gu_drained = pair("gu_full"), pair("gu_drained")
    th_done, sil_done, act_hi_done, act_split = sem("th_done"), sem("sil_done"), sem("act_hi_done"), sem("act_split")
    dn_full = [sem(f"dn_full{i}") for i in range(4)]
    acc_added = [sem(f"acc_added{i}") for i in range(4)]
    acc_zero, ssf_done, msf_ready, rstdf_ready = sem("acc_zero"), sem("ssf_done"), sem("msf_ready"), sem("rstdf_ready")
    yf_done, out_done, x1r_in, out_stored = sem("yf_done"), sem("out_done"), pair("x1r_in"), sem("out_stored")
    x1e_in = sem("x1e_in")
    end_done = sem("end_done")
    passed_pe, passed_dve, passed_sp, passed_pool = (sem(f"passed_{n}") for n in ("pe", "dve", "sp", "pool"))

    def rows(t):
        return bass.ds(t * P, P)

    def flat(ap):
        return ap.rearrange("p a n -> p (a n)")

    def chunk(c):
        return slice(c * P, (c + 1) * P)

    def passed(e, name):
        e.sem_inc(name, 1)

    def add_x1(e, s, done):
        if s < TILES - BT:
            e.wait_ge(x1r_in[s % 2], 16 * (s // 2 + 1))
            x1 = x1r[s % 2][:, :]
        else:
            e.wait_ge(x1e_in, 16)
            x1 = x1e[:, s % BT, :]
        e.wait_ge(yf_done, s + 1)
        e.tensor_tensor(acc[:, s % BT, :], acc[:, s % BT, :], x1, ALU.add).then_inc(done, 1)

    def use_h(k):
        return 3 * k + 1

    def use_q(k, last):
        return 3 * k + 2 - last

    def use_p(k, last):
        return 3 * k + 3 - last

    def over_tiles(e, body):
        body(0, 0, 0, 0, True)
        body(0, 1, 1, 0, True)
        with e.Fori(1, TILES // 2 - 1) as j:
            for par in range(2):
                body(j, par, 2, 0, True)
        body(TILES // 2 - 1, 0, 2, 0, False)
        body(TILES // 2 - 1, 1, 2, 1, False)

    PIECES = [(c, wq_hi, wq_lo, slice(0, QKV)) for c in range(KD)] + \
             [(c, wg_hi, wg_lo, slice(QKV, WIN)) for c in range(KD)]

    def piece(i):
        c, hi, lo, w = PIECES[i]
        return c, w, wraw[i % RAWS][:, 0:w.stop - w.start], hi[:, c, :], lo[:, c, :]

    gate_v = w_gate.rearrange("(k p) n -> p k n", p=P)
    up_v = w_up.rearrange("(k p) n -> p k n", p=P)
    down_v = w_down.rearrange("(g f p) n -> g p f n", f=2, p=P)
    gate_raw = raw_a[:, :].rearrange("p (k n) -> p k n", k=KD)
    up_raw = raw_b[:, :].rearrange("p (k n) -> p k n", k=KD)
    down_raw = raw_a[:, :].rearrange("p (f n) -> p f n", f=2)

    block = nc.Block()
    with block:
        @block.sync
        def _(e):
            e.dma_start(xt[0][:, :], x[0:P, :]).then_inc(x_in[0], 16)
            e.dma_start(gcol_in[:, :], gain_in).then_inc(gains_in, 16)
            for i in range(len(PIECES)):
                c, w, raw, hi, lo = piece(i)
                if i >= RAWS:
                    e.wait_ge(win_split, i + 1 - RAWS)
                e.dma_start(raw, w_in[chunk(c), w]).then_inc(wraw_in[i % RAWS], 16)
                if i == 3:
                    e.dma_start(xt[1][:, :], x[P:2 * P, :]).then_inc(x_in[1], 16)
                    e.dma_start(cs[:, 0:1, :], rope[:, 0:1, :]).then_inc(cs_in, 16)
            for dst, src in ((cs[:, 1:TILES, :], rope[:, 1:TILES, :]), (sgu_w[:, :, :], sgu_wt)):
                e.dma_start(dst, src).then_inc(consts, 16)
            for dst, src in ((sgub, sgu_bt), (sinkb, sinks), (lng, ln_g), (lnb, ln_b), (gcol_out, gain_out)):
                e.dma_start(dst[:, :], src).then_inc(consts, 16)
            for m in (2, 3):
                e.wait_ge(xn_done, m - 1)
                e.dma_start(xt[m % 2][:, :], x[m * P:(m + 1) * P, :]).then_inc(x_in[m % 2], 16)

            def tile(k, par, more):
                if more:
                    e.wait_ge(xn_done, k + 3)
                    e.dma_start(xt[par][:, :], x[rows(k + 4), :]).then_inc(x_in[par], 16)
                e.wait_ge(mix_done, 2 * k + 2)
                e.dma_start(mix_d[rows(k), :], mix[par][:, :]).then_inc(mix_out[par], 16)

            with e.Fori(0, TILES // 2 - 2) as j:
                for par in range(2):
                    tile(j * 2 + par, par, True)
            for k in range(TILES - 4, TILES - 2):
                tile(k, k % 2, False)

            e.wait_ge(zqkv_full, TILES)
            for c in range(KD):
                e.dma_start(wout_raw[c][:, :], w_out[chunk(c), :]).then_inc(wout_in[c], 16)
            for p in range(2):
                e.wait_ge(mix_out[p], 16 * (TILES // 2 - 1))
                e.dma_start(mixin[p][:, :], mix_d[p * P:(p + 1) * P, :]).then_inc(mix_in[p], 16)
            tile(TILES - 2, 0, False)
            e.wait_ge(zus_full, TILES)
            for p in range(2):
                e.wait_ge(rot_done, 2 * TILES)
                e.wait_ge(t_full[1], use_q(TILES - 1, 1) + 1)
                e.dma_start(xres[p][:, :], x[p * P:(p + 1) * P, :]).then_inc(xres_in[p], 16)
            e.dma_start(postm[:, :], post_mix).then_inc(posts, 16)
            e.dma_start(pref[:, :], pre_ffn).then_inc(posts, 16)
            e.wait_ge(mixT_full, 2)
            e.dma_start(mixin[0][:, :], mix_d[2 * P:3 * P, :]).then_inc(mix_in[0], 16)
            tile(TILES - 1, 1, False)

            def load_mix(k, par):
                e.wait_ge(mixT_full, 2 * k - 2)
                e.dma_start(mixin[par][:, :], mix_d[rows(k), :]).then_inc(mix_in[par], 16)

            def h2_store(k, src=h2s):
                e.wait_ge(h2s_split, 2 * k + 2)
                passed(e, passed_sp)
                for c in range(2):
                    e.dma_start(h2_d[:, c, :, rows(k)], src[:, c, :, :].bitcast(F32)).then_inc(h2_out, 16)

            def tile2(j, par, before, last, more):
                k = 2 * j + par
                if more:
                    load_mix(k + 3, 1 - par)
                if last:
                    e.wait_ge(mm2_full, TILES)
                    load_h2T(0, 1, (0,))
                e.wait_ge(x1_done, k + 1)
                e.dma_start(x1_d[rows(k), :], xres[par][:, :]).then_inc(x1_out[par], 16)
                if before:
                    h2_store(k - 1)
                    if not last:
                        e.wait_ge(h2n_done, k)
                        passed(e, passed_sp)
                        e.wait_ge(x1_out[1 - par], 16 * (j + par))
                        passed(e, passed_sp)
                        e.dma_start(xres[1 - par][:, :], x[rows(k + 1), :]).then_inc(xres_in[1 - par], 16)

            def load_gate(n, g):
                if not isinstance(n, int) or n:
                    e.wait_ge(wd_split, n)
                e.dma_start(gate_raw, gate_v[:, :, bass.ds(g * GW, GW)]).then_inc(gate_in, 16)

            def load_up(n, g):
                if not isinstance(n, int) or n:
                    e.wait_ge(up_split, 2 * n)
                e.dma_start(up_raw, up_v[:, :, bass.ds(g * GW, GW)]).then_inc(up_in, 16)

            def load_down(n, g):
                e.wait_ge(gate_split, 2 * n + 2)
                e.dma_start(down_raw, down_v[bass.ds(g, 1), :, :, :].rearrange("g p f n -> (g p) f n"))\
                    .then_inc(down_in, 16)

            def load_x1(s):
                if s >= 2:
                    e.wait_ge(out_done, s - 1)
                e.dma_start(x1r[s % 2][:, :], x1_d[rows(s), :]).then_inc(x1r_in[s % 2], 16)

            def load_h2T(b, h, parts=(0, 1)):
                for c in parts:
                    dst = (h2T_hi[h], h2T_lo[h])[c]
                    e.dma_start(dst[:, :, :].bitcast(F32), h2_d[:, c, :, b * BLK + h * 512:b * BLK + (h + 1) * 512])\
                        .then_inc(h2T_in[h], 16)

            tile2(0, 0, 0, 0, True)
            e.wait_ge(wout_split, KD)
            load_gate(0, 0)
            load_up(0, 0)
            tile2(0, 1, 1, 0, True)
            for p in range(2):
                e.wait_ge(mix_out[p], 16 * (TILES // 2))
            with e.Fori(1, TILES // 2 - 2) as j:
                for par in range(2):
                    tile2(j, par, 2, 0, True)
            tile2(TILES // 2 - 2, 0, 2, 0, True)
            tile2(TILES // 2 - 2, 1, 2, 0, False)
            e.wait_ge(h2_out, 32 * (TILES - 3))
            load_h2T(0, 0)
            tile2(TILES // 2 - 1, 0, 2, 0, False)
            tile2(TILES // 2 - 1, 1, 2, 1, False)
            e.wait_ge(h2n_done, TILES)
            for p in range(2):
                e.wait_ge(x1_out[p], 16 * (TILES // 2))
            load_h2T(0, 1, (1,))
            load_down(0, 0)
            h2_store(TILES - 1, h2s_end)
            e.wait_ge(h2_out, 32 * TILES)
            e.dma_start(postf[:, :], post_ffn).then_inc(post_in, 16)

            load_gate(1, 1)
            load_up(1, 1)
            for b in range(NB):
                with e.Fori(1 if b == 0 else 0, NG - 1) as g:
                    load_down(b * NG + g, g)
                    load_gate(b * NG + g + 1, g + 1)
                    load_up(b * NG + g + 1, g + 1)
                n = b * NG + NG - 1
                load_down(n, NG - 1)
                if b + 1 < NB:
                    load_x1(b * BT)
                    load_x1(b * BT + 1)
                    load_gate(n + 1, 0)
                    load_up(n + 1, 0)
                    e.wait_ge(gu_full[1], 2 * n + 1)
                    load_h2T(b + 1, 0)
                    e.wait_ge(gu_full[1], 2 * n + 2)
                    load_h2T(b + 1, 1)
                else:
                    e.wait_ge(gu_full[1], 2 * n + 1)
                    e.dma_start(x1e[:, :, :], x1_d[b * BLK:(b + 1) * BLK, :].rearrange("(t p) n -> p t n", p=P))\
                        .then_inc(x1e_in, 16)
                order = list(range(BT))
                if b + 1 == NB:
                    order[-3:] = [BT - 2, BT - 3, BT - 1]
                for t in order:
                    s = b * BT + t
                    if s < TILES - ENDS:
                        e.wait_ge(out_done, s + 1)
                    else:
                        e.wait_ge(end_done, s + 1 - (TILES - ENDS))
                    e.dma_start(out[rows(s), :], acc[:, t, :]).then_inc(out_stored, 16)
                    if b + 1 < NB and t + 2 < BT:
                        load_x1(s + 2)
            e.wait_ge(out_stored, 16 * TILES)

        @block.gpsimd
        def _(e):
            e.memset(ident[:, :], 0.0).then_inc(id_zero, 1)
            e.memset(mhalf[:, :], -0.5).then_inc(pool_consts, 1)
            e.memset(pbias[:, :], NEG).then_inc(pool_consts, 1)
            e.memset(kA[0][:, :], 0.0).then_inc(pool_consts, 1)
            e.memset(vA[0][:, :], 0.0).then_inc(pool_consts, 1)
            e.wait_ge(id_zero, 1)
            e.affine_select(out=ident[:, :], in_=ident[:, :], compare_op=ALU.not_equal, fill=1.0,
                            base=0, pattern=[[-1, P]], channel_multiplier=1).then_inc(pool_consts, 1)
            e.wait_ge(pool_consts, 5)

            def rstd_x(m, par):
                e.wait_ge(msx_ready, m + 1)
                e.tensor_tensor(rstdx[:, par:par + 1], msx[:, par:par + 1], mhalf[:, 0:1],
                                ALU.pow).then_inc(rstdx_ready, 1)

            def tile(j, par, before, last, ahead):
                k = 2 * j + par
                e.wait_ge(rope_mul, 3 * k + 3)
                if before:
                    e.wait_ge(t_full[0], 3 * k)
                    e.wait_ge(t_full[1], 3 * k)
                qv = "p (kv i d) -> p kv i d"
                e.tensor_tensor(qrot[:, :].rearrange("p (i kv d) -> p kv i d", kv=KVH, d=HD),
                                ropeA[:, 0:AW].rearrange(qv, kv=KVH, d=HD),
                                ropeB[:, 0:AW].rearrange(qv, kv=KVH, d=HD), ALU.add).then_inc(rot_done, 1)
                e.tensor_tensor(krot[:, :], ropeA[:, AW:AW + P], ropeB[:, AW:AW + P],
                                ALU.add).then_inc(rot_done, 1)
                if not before:
                    e.wait_ge(consts, 16 * 7)
                    e.wait_ge(rot_done, 2)
                    passed(e, passed_pool)
                    e.memset(sgu_w[CH:P, :, 0:CH], 0.0).then_inc(pool_consts, 1)
                    e.wait_ge(pool_consts, 6)
                if ahead:
                    rstd_x(k + 2, par)
                e.wait_ge(var_ready, k + 1)
                e.tensor_tensor(rstdv[:, :], varm[:, :], mhalf[:, 0:1], ALU.pow).then_inc(rstdv_ready, 1)
                e.wait_ge(vhat_done, k + 1)
                e.tensor_tensor(vn1[:, :], vhat[:, :], lng[:, :], ALU.mult).then_inc(vn1_done, 1)
                if before:
                    e.wait_ge(g_full, k)
                e.wait_ge(vn1_done, k + 1)
                e.tensor_tensor(vn[:, :], vn1[:, :], lnb[:, :], ALU.add).then_inc(vn_ready, 1)
                e.wait_ge(ms2_ready, k + 1)
                e.tensor_tensor(rs2[:, :], ms2[:, :], mhalf[:, 0:2], ALU.pow).then_inc(rs2_ready, 1)

            rstd_x(0, 0)
            rstd_x(1, 1)
            over_tiles(e, tile)

            def tile2(j, par, before, last, ahead):
                k = 2 * j + par
                e.wait_ge(msm_ready, k + 1)
                e.tensor_tensor(rstdm[:, par:par + 1], msm[:, par:par + 1], mhalf[:, 0:1],
                                ALU.pow).then_inc(rstdm_ready, 1)
                e.wait_ge(msy_ready, k + 1)
                e.tensor_tensor(rstdy[:, par:par + 1], msy[:, par:par + 1], mhalf[:, 0:1],
                                ALU.pow).then_inc(rstdy_ready, 1)

            over_tiles(e, tile2)

            for b in range(NB):
                e.wait_ge(mm2_full, TILES)
                if b == 0:
                    e.wait_ge(h2_out, 32 * TILES)
                else:
                    e.wait_ge(out_stored, 16 * b * BT)
                e.memset(acc[:, :, :], 0.0).then_inc(acc_zero, 1)
                for t in range(BT):
                    s = b * BT + t
                    e.wait_ge(msf_ready, s + 1)
                    e.tensor_tensor(rstdf[:, t:t + 1], msf[:, t:t + 1], mhalf[:, 0:1], ALU.pow).then_inc(rstdf_ready, 1)
                    if t >= 2:
                        add_x1(e, s - 2, out_done)
                if b + 1 < NB:
                    for s in range(b * BT + BT - 2, b * BT + BT):
                        add_x1(e, s, out_done)

        @block.scalar
        def _(e):
            def stats_x(m, j, par):
                e.wait_ge(x_in[par], 16 * (j + 1))
                e.activation(squares1[:, :], xt[par][:, :], ACT.Square,
                             accum_out=ssx[:, par:par + 1]).then_inc(ssx_done, 1)
                e.wait_ge(ssx_done, m + 1)
                e.activation(msx[:, par:par + 1], ssx[:, par:par + 1], ACT.Copy, scale=1.0 / D,
                             bias=EPS).then_inc(msx_ready, 1)

            def h_hi(par, use):
                for i in range(2):
                    e.wait_ge(t_full[i], use + 1)
                    e.activation(hT_hi[par][:, i * 512:(i + 1) * 512], T[i][:, :], ACT.Copy).then_inc(h_hi_done, 1)

            def tile(j, par, before, last, ahead):
                k = 2 * j + par
                if not last:
                    h_hi(1 - par, use_h(k))
                e.wait_ge(rope_mul, 3 * k + 3)
                if before:
                    e.wait_ge(pv_done, k)
                e.activation(vB[:, :], ZA[:, 1, P:2 * P], ACT.Copy).then_inc(v_done, 1)
                e.activation(vA[par][0:CH, :], ZA[0:CH, 1, P:2 * P], ACT.Copy).then_inc(v_done, 1)
                e.activation(vA[1 - par][CH:P, :], ZA[CH:P, 1, P:2 * P], ACT.Copy).then_inc(v_done, 1)
                if ahead:
                    stats_x(k + 2, j + 1, par)
                e.wait_ge(t_full[0], use_q(k, last) + 1)
                e.activation(qT[:, :], T0[:, :], ACT.Copy).then_inc(t_drained[0], 1)
                if last:
                    wout_hi_parts(0, KD // 2)
                e.wait_ge(zus_full, k + 1)
                if before:
                    e.wait_ge(sB_done, k)
                e.activation(gel[:, :], flat(ZB[:, :, :]), ACT.Gelu).then_inc(gel_done, 1)
                if last:
                    mix_hi(0, 0)
                e.wait_ge(soft_ready, 2 * k + 2)
                e.activation(esink[:, :], dsink[:, :], ACT.Exp).then_inc(exp_done, 1)
                for h in range(NH):
                    e.activation(probs[:, chunk(h)], S[:, h // PAIRS, chunk(h % PAIRS)],
                                 ACT.Exp, bias=mneg[:, h:h + 1], scale=HD ** -0.5,
                                 accum_out=den[:, h:h + 1]).then_inc(exp_done, 1)
                if last:
                    wout_hi_parts(KD // 2, KD // 2 + 2)
                e.wait_ge(t_full[0], use_p(k, last) + 1)
                e.activation(probsT[:, 0:512], T0[:, :], ACT.Copy).then_inc(t_drained[0], 1)
                if last:
                    wout_hi_parts(KD // 2 + 2, KD)
                    mix_hi(1, 1)
                e.wait_ge(sB_done, k + 1)
                e.activation(squares1[:, AW:D], sB[:, :], ACT.Square, accum_out=ss2[:, 1:2]).then_inc(ss2_done, 1)
                e.wait_ge(aO_done, k + 1)
                e.activation(squares1[:, 0:AW], aO[:, :], ACT.Square, accum_out=ss2[:, 0:1]).then_inc(ss2_done, 1)
                e.wait_ge(ss2_done, 2 * k + 2)
                e.activation(ms2[:, :], ss2[:, :], ACT.Copy, scale=1.0 / SW, bias=EPS).then_inc(ms2_ready, 1)

            def wout_hi_parts(first, end):
                if first == 0:
                    e.wait_ge(zqkv_full, TILES)
                else:
                    e.wait_ge(zus_full, TILES)
                e.wait_ge(consts, 16 * 7)
                for c in range(first, end):
                    e.wait_ge(wout_in[c], 16)
                    e.activation(wout_hi[:, c, :], wout_raw[c][:, :], ACT.Copy,
                                 scale=gcol_out[:, c:c + 1]).then_inc(wout_hi_done, 1)

            def mix_hi(k, par):
                for i in range(2):
                    e.wait_ge(mixT_full, 2 * k + i + 1)
                    e.activation(mixT_hi[par][:, i * 512:(i + 1) * 512], T[i][:, :], ACT.Copy).then_inc(mixT_hi_done, 1)

            stats_x(0, 0, 0)
            e.wait_ge(gains_in, 16)
            for i in range(len(PIECES)):
                c, w, raw, hi, lo = piece(i)
                e.wait_ge(wraw_in[i % RAWS], 16 * (i // RAWS + 1))
                e.activation(hi, raw, ACT.Copy, scale=gcol_in[:, c:c + 1]).then_inc(win_hi_done, 1)
                if i == 1:
                    h_hi(0, 0)
                if i == 5:
                    stats_x(1, 0, 1)
            e.wait_ge(pool_consts, 5)
            over_tiles(e, tile)

            def h2_hi(k, first, dst=h2s):
                if not first:
                    e.wait_ge(h2_out, 32 * k)
                for i in range(2):
                    e.wait_ge(h2T_full, 2 * k + i + 1)
                    e.activation(flat(dst[:, 0, 4 * i:4 * i + 4, :]), S[:, i, :], ACT.Copy).then_inc(h2s_hi_done, 1)

            def tile2(j, par, before, last, ahead):
                k = 2 * j + par
                if not last and before:
                    mix_hi(k + 1, 1 - par)
                e.wait_ge(mm2_full, k + 1)
                e.activation(squares2[:, :], flat(M[par][:, :, :]), ACT.Square,
                             accum_out=ssm[:, par:par + 1]).then_inc(ssm_done, 1)
                e.wait_ge(ssm_done, k + 1)
                e.activation(msm[:, par:par + 1], ssm[:, par:par + 1], ACT.Copy, scale=1.0 / D,
                             bias=EPS).then_inc(msm_ready, 1)
                if before:
                    h2_hi(k - 1, before == 1)
                e.wait_ge(x1_done, k + 1)
                e.activation(squares2[:, :], xres[par][:, :], ACT.Square,
                             accum_out=ssy[:, par:par + 1]).then_inc(ssy_done, 1)
                e.wait_ge(ssy_done, k + 1)
                e.activation(msy[:, par:par + 1], ssy[:, par:par + 1], ACT.Copy, scale=1.0 / D,
                             bias=EPS).then_inc(msy_ready, 1)

            def gate_up_hi(n, f):
                if not isinstance(n, int) or n:
                    e.wait_ge(gu_full[f], 2 * n)
                e.wait_ge(gate_in, 16 * n + 16)
                e.activation(gu_hi[f][:, 0], gate_raw[:, :, chunk(f)], ACT.Copy).then_inc(gu_hi_done, 1)
                e.wait_ge(up_in, 16 * n + 16)
                e.activation(gu_hi[f][:, 1], up_raw[:, :, chunk(f)], ACT.Copy).then_inc(gu_hi_done, 1)

            tile2(0, 0, 0, 0, True)
            tile2(0, 1, 1, 0, True)
            with e.Fori(1, TILES // 2 - 1) as j:
                for par in range(2):
                    tile2(j, par, 2, 0, True)
            gate_up_hi(0, 0)
            tile2(TILES // 2 - 1, 0, 2, 0, False)
            gate_up_hi(0, 1)
            tile2(TILES // 2 - 1, 1, 2, 1, False)

            def unit(n, q):
                h, f = q // 2, q % 2
                e.wait_ge(gu_full[f], 2 * n + h + 1)
                e.activation(th[f][:, :], GU[f][:, 0, :], ACT.Tanh, scale=0.5).then_inc(th_done, 1)
                e.wait_ge(gu_drained[f], 2 * n + h + 1)
                if q == 0 and (not isinstance(n, int) or n):
                    e.wait_ge(dn_full[3], 4 * n)
                e.activation(act_hi[:, f, h * 512:(h + 1) * 512], prod[f][:, :], ACT.Copy,
                             scale=0.5).then_inc(act_hi_done, 1)

            def down_hi(n):
                if not isinstance(n, int) or n:
                    e.wait_ge(dn_full[3], 4 * n)
                e.wait_ge(down_in, 16 * n + 16)
                e.activation(flat(wd_hi[:, :, :]), raw_a[:, :], ACT.Copy).then_inc(wd_hi_done, 1)

            def group(n, more=True):
                unit(n, 0)
                if isinstance(n, int) and n == 0:
                    h2_hi(TILES - 1, True, h2s_end)
                unit(n, 1)
                down_hi(n)
                unit(n, 2)
                if more:
                    gate_up_hi(n + 1, 0)
                unit(n, 3)
                if more:
                    gate_up_hi(n + 1, 1)

            group(0)
            for b in range(NB):
                with e.Fori(1 if b == 0 else 0, NG - 1) as g:
                    group(b * NG + g)
                n = b * NG + NG - 1
                group(n, b + 1 < NB)
                for t in range(BT):
                    s = b * BT + t
                    for i in range(2):
                        e.wait_ge(acc_added[(2 * t + i) % 4], 4 * n + (2 * t + i) // 4 + 1)
                    e.activation(squares3[:, :], acc[:, t, :], ACT.Square,
                                 accum_out=ssf[:, t:t + 1]).then_inc(ssf_done, 1)
                    e.wait_ge(ssf_done, s + 1)
                    e.activation(msf[:, t:t + 1], ssf[:, t:t + 1], ACT.Copy, scale=1.0 / D,
                                 bias=EPS).then_inc(msf_ready, 1)

        @block.vector
        def _(e):
            def norm_x(m, par):
                e.wait_ge(rstdx_ready, m + 1)
                if not isinstance(m, int) or m:
                    e.wait_ge(t_full[1], 1 if isinstance(m, int) and m == 1 else 3 * m - 4)
                e.tensor_scalar(xn[:, :], xt[par][:, :], rstdx[:, par:par + 1], None,
                                ALU.mult).then_inc(xn_done, 1)

            def h_lo(par, m):
                for i in range(2):
                    e.wait_ge(h_hi_done, 2 * m + i + 1)
                    half = slice(i * 512, (i + 1) * 512)
                    e.tensor_tensor(hT_lo[par][:, half], T[i][:, :], hT_hi[par][:, half].bitcast(F32),
                                    ALU.subtract).then_inc(t_drained[i], 1)

            def rope_products(m):
                e.wait_ge(zqkv_full, m + 1)
                if not isinstance(m, int) or m:
                    e.wait_ge(rot_done, 2 * m)
                z = flat(ZA[:, :, :])[:, 0:AW + P]
                c = cs[:, bass.ds(m, 1), :]
                e.tensor_tensor(ropeA[:, :].rearrange("p (h d) -> p h d", d=32), z.rearrange("p (h d) -> p h d", d=32),
                                c[:, :, 0:32].to_broadcast([P, 20, 32]), ALU.mult).then_inc(rope_mul, 1)
                zz = z.rearrange("p (h t d) -> p h t d", t=2, d=32)
                rb = ropeB[:, :].rearrange("p (h t d) -> p h t d", t=2, d=32)
                for a in range(2):
                    e.tensor_tensor(rb[:, :, a, :], zz[:, :, 1 - a, :],
                                    c[:, :, 32 + 32 * a:64 + 32 * a].to_broadcast([P, 10, 32]),
                                    ALU.mult).then_inc(rope_mul, 1)

            def tile(j, par, before, last, ahead):
                k = 2 * j + par
                if not last:
                    h_lo(1 - par, k + 1)
                e.wait_ge(t_full[1], use_q(k, last) + 1)
                e.tensor_copy(kB[:, :], T1[:, 0:P]).then_inc(k_done, 1)
                e.tensor_copy(kA[par][:, 0:CH], T1[:, 0:CH]).then_inc(k_done, 1)
                e.tensor_copy(kA[1 - par][:, CH:P], T1[:, CH:P]).then_inc(t_drained[1], 1)
                if last:
                    e.wait_ge(zus_full, TILES)
                    wout_lo_parts(0, 1)
                    mix_lo(0, 0)
                    wout_lo_parts(1, 2)
                e.wait_ge(s_full, k + 1)
                first_q = S[0:CH, :, :].rearrange("p a (h n) -> p (a h) n", n=P)[:, :, CH:P]
                if not before:
                    e.wait_ge(consts, 16 * 7)
                    e.tensor_scalar(first_q, first_q, pbias[0:CH, 0:1], None, ALU.add).then_inc(masked, 1)
                    e.wait_ge(masked, 1)
                e.tensor_reduce(mraw[:, :], S[:, :, :].rearrange("p a (h n) -> p (a h) n", n=P), AX_X,
                                ALU.max).then_inc(mraw_done, 1)
                e.wait_ge(mraw_done, k + 1)
                e.scalar_tensor_tensor(out=mtop[:, :], in0=mraw[:, :], scalar=HD ** -0.5, in1=sinkb[:, :],
                                       op0=ALU.mult, op1=ALU.max).then_inc(mtop_done, 1)
                e.wait_ge(mtop_done, k + 1)
                e.tensor_scalar(mneg[:, :], mtop[:, :], -1.0, None, ALU.mult).then_inc(soft_ready, 1)
                e.tensor_tensor(dsink[:, :], sinkb[:, :], mtop[:, :], ALU.subtract).then_inc(soft_ready, 1)
                e.wait_ge(gel_done, k + 1)
                e.bn_stats(st6[:, :], gel[:, SW:2 * SW]).then_inc(st6_done, 1)
                if ahead:
                    norm_x(k + 2, par)
                e.wait_ge(st6_done, k + 1)
                passed(e, passed_dve)
                e.bn_aggr(mv[:, :], st6[:, :]).then_inc(mv_done, 1)
                e.wait_ge(mv_done, k + 1)
                e.tensor_scalar(varm[:, :], mv[:, 1:2], EPS, None, ALU.add).then_inc(var_ready, 1)
                if last:
                    wout_lo_parts(2, 3)
                e.wait_ge(rstdv_ready, k + 1)
                e.tensor_scalar(vhat[:, :], gel[:, SW:2 * SW], mv[:, 0:1], rstdv[:, 0:1], ALU.subtract,
                                ALU.mult).then_inc(vhat_done, 1)
                if last:
                    wout_lo_parts(3, KD // 2)
                e.wait_ge(exp_done, 9 * k + 9)
                e.tensor_tensor(dtot[:, :], den[:, :], esink[:, :], ALU.add).then_inc(dtot_done, 1)
                e.wait_ge(dtot_done, k + 1)
                e.reciprocal(rden[:, :], dtot[:, :]).then_inc(rden_done, 1)
                if last:
                    wout_lo_parts(KD // 2, KD // 2 + 2)
                e.wait_ge(t_full[1], use_p(k, last) + 1)
                e.tensor_copy(probsT[:, 512:1024], T1[:, :]).then_inc(t_drained[1], 1)
                if last:
                    wout_lo_parts(KD // 2 + 2, KD)
                    mix_lo(1, 1)
                else:
                    rope_products(k + 1)
                e.wait_ge(g_full, k + 1)
                for g in range(SG):
                    ins = e.scalar_tensor_tensor(out=sB[:, chunk(g)], in0=S[:, 1, chunk(g)], scalar=sgub[:, g:g + 1],
                                                 in1=gel[:, chunk(g)], op0=ALU.add, op1=ALU.mult)
                ins.then_inc(sB_done, 1)
                e.wait_ge(pv_done, k + 1)
                e.wait_ge(rden_done, k + 1)
                e.tensor_tensor(aO[:, :].rearrange("p (h d) -> p h d", d=HD),
                                S[:, 0, :].rearrange("p (h d) -> p h d", d=HD),
                                rden[:, :].unsqueeze(2).to_broadcast([P, NH, HD]), ALU.mult).then_inc(aO_done, 1)
                if before == 2:
                    e.wait_ge(mix_out[par], 16 * j)
                e.wait_ge(rs2_ready, k + 1)
                e.tensor_scalar(mix[par][:, AW:D], sB[:, :], rs2[:, 1:2], None, ALU.mult).then_inc(mix_done, 1)
                e.tensor_scalar(mix[par][:, 0:AW], aO[:, :], rs2[:, 0:1], None, ALU.mult).then_inc(mix_done, 1)

            def wout_lo_parts(first, end):
                for c in range(first, end):
                    e.wait_ge(wout_hi_done, c + 1)
                    e.scalar_tensor_tensor(out=wout_lo[:, c, :], in0=wout_raw[c][:, :], scalar=gcol_out[:, c:c + 1],
                                           in1=wout_hi[:, c, :].bitcast(F32), op0=ALU.mult,
                                           op1=ALU.subtract).then_inc(wout_split, 1)

            def mix_lo(k, par):
                for i in range(2):
                    e.wait_ge(mixT_hi_done, 2 * k + i + 1)
                    half = slice(i * 512, (i + 1) * 512)
                    e.tensor_tensor(mixT_lo[par][:, half], T[i][:, :], mixT_hi[par][:, half].bitcast(F32),
                                    ALU.subtract).then_inc(mixT_split, 1)

            norm_x(0, 0)
            e.wait_ge(gains_in, 16)
            for i in range(len(PIECES)):
                c, w, raw, hi, lo = piece(i)
                e.wait_ge(win_hi_done, i + 1)
                e.scalar_tensor_tensor(out=lo, in0=raw, scalar=gcol_in[:, c:c + 1],
                                       in1=hi.bitcast(F32), op0=ALU.mult,
                                       op1=ALU.subtract).then_inc(win_split, 1)
                if i == 1:
                    h_lo(0, 0)
                if i == 5:
                    norm_x(1, 1)
                if i == 12:
                    e.wait_ge(cs_in, 16)
                    rope_products(0)
            e.wait_ge(pool_consts, 5)
            over_tiles(e, tile)

            e.wait_ge(posts, 32)

            def h2_lo(k, dst=h2s):
                for i in range(2):
                    e.wait_ge(h2s_hi_done, 2 * k + i + 1)
                    ks = slice(4 * i, 4 * i + 4)
                    e.tensor_tensor(flat(dst[:, 1, ks, :]), S[:, i, :], flat(dst[:, 0, ks, :]).bitcast(F32),
                                    ALU.subtract).then_inc(h2s_split, 1)

            def tile2(j, par, before, last, ahead):
                k = 2 * j + par
                if not last and before:
                    mix_lo(k + 1, 1 - par)
                e.wait_ge(rstdm_ready, k + 1)
                e.scalar_tensor_tensor(out=ytmp[:, :], in0=flat(M[par][:, :, :]), scalar=rstdm[:, par:par + 1],
                                       in1=postm[:, :], op0=ALU.mult, op1=ALU.mult).then_inc(y_done, 1)
                e.wait_ge(xres_in[par], 16 * (j + 1))
                e.wait_ge(y_done, k + 1)
                e.tensor_tensor(xres[par][:, :], ytmp[:, :], xres[par][:, :], ALU.add).then_inc(x1_done, 1)
                if before:
                    h2_lo(k - 1)
                    e.wait_ge(h2T_full, 2 * k)
                e.wait_ge(rstdy_ready, k + 1)
                e.scalar_tensor_tensor(out=h2n[:, :], in0=xres[par][:, :], scalar=rstdy[:, par:par + 1],
                                       in1=pref[:, :], op0=ALU.mult, op1=ALU.mult).then_inc(h2n_done, 1)

            def gate_up_lo(n, f):
                for c, (raw, done) in enumerate(((gate_raw, gate_split), (up_raw, up_split))):
                    e.wait_ge(gu_hi_done, 4 * n + 2 * f + c + 1)
                    e.tensor_tensor(gu_lo[f][:, c], raw[:, :, chunk(f)], gu_hi[f][:, c].bitcast(F32),
                                    ALU.subtract).then_inc(done, 1)

            tile2(0, 0, 0, 0, True)
            tile2(0, 1, 1, 0, True)
            with e.Fori(1, TILES // 2 - 1) as j:
                for par in range(2):
                    tile2(j, par, 2, 0, True)
            gate_up_lo(0, 0)
            tile2(TILES // 2 - 1, 0, 2, 0, False)
            gate_up_lo(0, 1)
            tile2(TILES // 2 - 1, 1, 2, 1, False)

            def unit(n, q):
                h, f = q // 2, q % 2
                e.wait_ge(th_done, 4 * n + q + 1)
                e.scalar_tensor_tensor(out=sil[f][:, :], in0=th[f][:, :], scalar=1.0, in1=GU[f][:, 0, :],
                                       op0=ALU.add, op1=ALU.mult).then_inc(sil_done, 1)
                e.wait_ge(sil_done, 4 * n + q + 1)
                e.tensor_tensor(prod[f][:, :], sil[f][:, :], GU[f][:, 1, :], ALU.mult).then_inc(gu_drained[f], 1)
                e.wait_ge(act_hi_done, 4 * n + q + 1)
                half = slice(h * 512, (h + 1) * 512)
                e.scalar_tensor_tensor(out=act_lo[:, f, half], in0=prod[f][:, :], scalar=0.5,
                                       in1=act_hi[:, f, half].bitcast(F32), op0=ALU.mult,
                                       op1=ALU.subtract).then_inc(act_split, 1)

            def down_lo(n):
                e.wait_ge(wd_hi_done, n + 1)
                e.tensor_tensor(flat(wd_lo[:, :, :]), raw_a[:, :], flat(wd_hi[:, :, :]).bitcast(F32),
                                ALU.subtract).then_inc(wd_split, 1)

            def scale_out(b, t):
                e.wait_ge(rstdf_ready, b * BT + t + 1)
                e.scalar_tensor_tensor(out=acc[:, t, :], in0=acc[:, t, :], scalar=rstdf[:, t:t + 1],
                                       in1=postf[:, :], op0=ALU.mult, op1=ALU.mult).then_inc(yf_done, 1)

            def group(n, b, end=False, more=True):
                unit(n, 0)
                if isinstance(n, int) and n == 0:
                    h2_lo(TILES - 1, h2s_end)
                unit(n, 1)
                down_lo(n)
                unit(n, 2)
                if more:
                    gate_up_lo(n + 1, 0)
                unit(n, 3)
                e.wait_ge(acc_zero, b + 1)
                for i in range(2 * BT):
                    t, d = i // 2, i % 2
                    if i == 4 and more:
                        gate_up_lo(n + 1, 1)
                    e.wait_ge(dn_full[i % 4], 4 * n + i // 4 + 1)
                    a = acc[:, t, d * 512:(d + 1) * 512]
                    e.tensor_tensor(a, DN[i % 4], a, ALU.add).then_inc(acc_added[i % 4], 1)
                    if end and i == 2:
                        e.wait_ge(post_in, 16)
                    if end and t >= 2 and d:
                        scale_out(b, t - 2)
                if end:
                    scale_out(b, BT - 2)
                    if not more:
                        add_x1(e, TILES - 2, end_done)
                    scale_out(b, BT - 1)
                    if not more:
                        add_x1(e, TILES - 1, end_done)

            group(0, 0)
            for b in range(NB):
                with e.Fori(1 if b == 0 else 0, NG - 1) as g:
                    group(b * NG + g, b)
                group(b * NG + NG - 1, b, end=True, more=b + 1 < NB)

        @block.tensor
        def _(e):
            def three(out_ap, lhi, llo, rhi, rlo, start, stop):
                e.matmul(out_ap, lhi, rhi, start=start, stop=False)
                e.matmul(out_ap, lhi, rlo, start=False, stop=False)
                return e.matmul(out_ap, llo, rhi, start=False, stop=stop)

            def h_transposes(m, use):
                e.wait_ge(xn_done, m + 1)
                for i in range(2):
                    if not isinstance(use, int) or use:
                        e.wait_ge(t_drained[i], use)
                    for c in range(4):
                        ins = e.transpose(T[i][:, chunk(c)], xn[:, chunk(4 * i + c)], ident[:, :])
                    ins.then_inc(t_full[i], 1)

            def z_columns(out_ap, par, hi, lo, w):
                for c in range(KD):
                    ins = three(out_ap, hT_hi[par][:, chunk(c)], hT_lo[par][:, chunk(c)], hi[:, c, w],
                                lo[:, c, w], c == 0, c == KD - 1)
                return ins

            def z_first(parts, pieces):
                for c in range(KD):
                    e.wait_ge(win_split, pieces + c + 1)
                    for out_ap, hi, lo, w in parts:
                        ins = three(out_ap, hT_hi[0][:, chunk(c)], hT_lo[0][:, chunk(c)], hi[:, c, w],
                                    lo[:, c, w], c == 0, c == KD - 1)
                return ins

            def z_qkv(m, par, use):
                for i in range(2):
                    e.wait_ge(t_drained[i], use + 1)
                e.wait_ge(rope_mul, 3 * m)
                e.wait_ge(v_done, 3 * m)
                z_columns(ZA[:, 0, :], par, wq_hi, wq_lo, slice(0, AW))
                z_columns(ZA[:, 1, 0:2 * P], par, wq_hi, wq_lo, slice(AW, QKV)).then_inc(zqkv_full, 1)

            def mix_transposes(k, j, par):
                e.wait_ge(mix_in[par], 16 * (j + 1))
                if not isinstance(k, int) or k:
                    e.wait_ge(mixT_split, 2 * k)
                for i in range(2):
                    for c in range(4):
                        ins = e.transpose(T[i][:, chunk(c)], mixin[par][:, chunk(4 * i + c)], ident[:, :])
                    ins.then_inc(mixT_full, 1)

            def first_products(first, end):
                for c in range(first, end):
                    e.wait_ge(wout_split, c + 1)
                    for a in range(2):
                        w = slice(a * 512, (a + 1) * 512)
                        ins = three(M[0][:, a, :], mixT_hi[0][:, chunk(c)], mixT_lo[0][:, chunk(c)],
                                    wout_hi[:, c, w], wout_lo[:, c, w], c == 0, c == KD - 1)
                return ins

            def tile(j, par, before, last, ahead):
                k = 2 * j + par
                if not last:
                    h_transposes(k + 1, use_h(k))
                if before:
                    e.wait_ge(gel_done, k)
                    z_columns(ZB[:, 0, :], par, wg_hi, wg_lo, slice(0, SW))
                else:
                    z_first([(ZB[:, a, :], wg_hi, wg_lo, slice(a * SW, (a + 1) * SW)) for a in range(2)],
                            KD).then_inc(zus_full, 1)
                e.wait_ge(rot_done, 2 * k + 2)
                e.wait_ge(t_drained[0], use_q(k, last))
                for i in range(PAIRS):
                    ins = e.transpose(T0[:, chunk(i)], qrot[:, chunk(i)], ident[:, :])
                ins.then_inc(t_full[0], 1)
                e.wait_ge(t_drained[1], use_q(k, last))
                e.transpose(T1[:, 0:P], krot[:, :], ident[:, :]).then_inc(t_full[1], 1)
                if before:
                    z_columns(ZB[:, 1, :], par, wg_hi, wg_lo, slice(SW, 2 * SW)).then_inc(zus_full, 1)
                e.wait_ge(t_drained[0], use_q(k, last) + 1)
                e.wait_ge(t_drained[1], use_q(k, last) + 1)
                if last:
                    mix_transposes(0, 0, 0)
                e.wait_ge(k_done, 2 * k + 2)
                if before:
                    e.wait_ge(aO_done, k)
                    e.wait_ge(sB_done, k)
                passed(e, passed_pe)
                for i in range(PAIRS):
                    for half, keys in enumerate((kA[par], kB)):
                        for kv in range(KVH):
                            r = slice(kv * HD, (kv + 1) * HD)
                            ins = e.matmul(S[half * CH:(half + 1) * CH, kv, chunk(i)],
                                           qT[r, i * P + half * CH:i * P + (half + 1) * CH], keys[r, :],
                                           start=True, stop=True)
                ins.then_inc(s_full, 1)
                if not last:
                    z_qkv(k + 1, 1 - par, use_h(k))
                else:
                    e.wait_ge(mixT_split, 2)
                    first_products(0, KD // 2)
                e.wait_ge(exp_done, 9 * k + 9)
                for i in range(2):
                    e.wait_ge(t_drained[i], use_p(k, last))
                    for c in range(4):
                        ins = e.transpose(T[i][:, chunk(c)], probs[:, chunk(4 * i + c)], ident[:, :])
                    ins.then_inc(t_full[i], 1)
                if not before:
                    e.wait_ge(pool_consts, 6)
                e.wait_ge(vn_ready, k + 1)
                for g in range(SG):
                    ins = e.matmul(S[:, 1, chunk(g)], sgu_w[:, g, :], vn[:, chunk(g)], start=True, stop=True)
                ins.then_inc(g_full, 1)
                e.wait_ge(t_drained[0], use_p(k, last) + 1)
                e.wait_ge(t_drained[1], use_p(k, last) + 1)
                e.wait_ge(v_done, 3 * k + 3)
                for h in range(NH):
                    kv = h // PAIRS
                    for half, vals in enumerate((vA[par], vB)):
                        ins = e.matmul(S[half * CH:(half + 1) * CH, 0, h * HD:(h + 1) * HD],
                                       probsT[:, h * P + half * CH:h * P + (half + 1) * CH],
                                       vals[:, kv * HD:(kv + 1) * HD], start=True, stop=True)
                ins.then_inc(pv_done, 1)

            e.wait_ge(pool_consts, 5)
            h_transposes(0, 0)
            for i in range(2):
                e.wait_ge(t_drained[i], 1)
            z_first([(ZA[:, 0, :], wq_hi, wq_lo, slice(0, AW)), (ZA[:, 1, 0:2 * P], wq_hi, wq_lo, slice(AW, QKV))],
                    0).then_inc(zqkv_full, 1)
            over_tiles(e, tile)

            def h2_transposes(k, first=False):
                e.wait_ge(h2n_done, k + 1)
                if not first:
                    e.wait_ge(h2s_split, 2 * k)
                for i in range(2):
                    for c in range(4):
                        ins = e.transpose(S[:, i, chunk(c)], h2n[:, chunk(4 * i + c)], ident[:, :])
                    ins.then_inc(h2T_full, 1)

            def tile2(j, par, before, last, ahead):
                k = 2 * j + par
                if not last:
                    mix_transposes(k + 1, j + par, 1 - par)
                e.wait_ge(mixT_split, 2 * k + 2)
                if before == 2:
                    e.wait_ge(y_done, k - 1)
                if before == 0:
                    ins = first_products(KD // 2, KD)
                else:
                    for a in range(2):
                        for c in range(KD):
                            w = slice(a * 512, (a + 1) * 512)
                            ins = three(M[par][:, a, :], mixT_hi[par][:, chunk(c)], mixT_lo[par][:, chunk(c)],
                                        wout_hi[:, c, w], wout_lo[:, c, w], c == 0, c == KD - 1)
                ins.then_inc(mm2_full, 1)
                if before:
                    if before == 1:
                        e.wait_ge(aO_done, TILES)
                    h2_transposes(k - 1, before == 1)

            over_tiles(e, tile2)

            def group(n, b):
                for q in range(4):
                    h, f = q // 2, q % 2
                    if h == 0:
                        e.wait_ge(gate_split, 2 * n + f + 1)
                        e.wait_ge(up_split, 2 * n + f + 1)
                    if not (isinstance(n, int) and n == 0 and h == 0):
                        e.wait_ge(gu_drained[f], 2 * n + h)
                    e.wait_ge(h2T_in[h], 32 * (b + 1))
                    for a in range(2):
                        for c in range(KD):
                            ins = three(GU[f][:, a, :], gu_hi[f][:, a, c, :], gu_lo[f][:, a, c, :],
                                        h2T_hi[h][:, c, :], h2T_lo[h][:, c, :], c == 0, c == KD - 1)
                    ins.then_inc(gu_full[f], 1)
                    if isinstance(n, int) and n == 0 and q == 0:
                        h2_transposes(TILES - 1)
                e.wait_ge(wd_split, n + 1)
                for i in range(2 * BT):
                    t, d = i // 2, i % 2
                    if i == 0:
                        e.wait_ge(act_split, 4 * n + 2)
                    if i == BT:
                        e.wait_ge(act_split, 4 * n + 4)
                    if not (isinstance(n, int) and n == 0 and i < 4):
                        e.wait_ge(acc_added[i % 4], 4 * n + i // 4)
                    for f in range(2):
                        w = slice(d * 512, (d + 1) * 512)
                        ins = three(DN[i % 4], act_hi[:, f, chunk(t)], act_lo[:, f, chunk(t)], wd_hi[:, f, w],
                                    wd_lo[:, f, w], f == 0, f == 1)
                    ins.then_inc(dn_full[i % 4], 1)

            e.wait_ge(y_done, TILES - 1)
            group(0, 0)
            for b in range(NB):
                with e.Fori(1 if b == 0 else 0, NG - 1) as g:
                    group(b * NG + g, b)
                group(b * NG + NG - 1, b)


def rope_table():
    inv = np.float32(1) / (10000.0 ** (np.arange(0, HD, 2) / HD)).astype(np.float32)
    ang = (np.arange(SEQ, dtype=np.float32)[:, None] * inv[None, :]).astype(np.float32).astype(np.float64)
    t = np.concatenate([np.cos(ang), -np.sin(ang), np.sin(ang)], axis=1).astype(np.float32)
    return np.ascontiguousarray(t.reshape(TILES, P, 96).transpose(1, 0, 2))


def kernel(x, norm_mix_pre, norm_mix_post, w_in, attn_sinks, sgu_ln_g, sgu_ln_b, sgu_w, sgu_b,
           norm_out_attn, norm_out_sgu, w_out, norm_ffn_pre, norm_ffn_post, w_gate, w_up, w_down):
    import concourse.bacc as bacc
    from concourse.bass_utils import run_bass_kernel_spmd

    def cols(*v):
        return np.concatenate([np.asarray(a)[0] for a in v]).reshape(KD, P).T

    def bcast(v):
        return np.broadcast_to(np.asarray(v)[0], (P, np.asarray(v).shape[1]))

    arrays = {
        "x": np.asarray(x)[0], "w_in": np.asarray(w_in)[0], "w_out": np.asarray(w_out)[0],
        "w_gate": np.asarray(w_gate)[0], "w_up": np.asarray(w_up)[0], "w_down": np.asarray(w_down)[0],
        "gain_in": cols(norm_mix_pre), "gain_out": cols(norm_out_attn, norm_out_sgu),
        "post_mix": bcast(norm_mix_post), "pre_ffn": bcast(norm_ffn_pre), "post_ffn": bcast(norm_ffn_post),
        "sinks": bcast(attn_sinks), "ln_g": bcast(sgu_ln_g), "ln_b": bcast(sgu_ln_b),
        "sgu_wt": np.asarray(sgu_w)[0].transpose(2, 0, 1), "sgu_bt": np.asarray(sgu_b)[0].T,
        "rope": rope_table(),
    }
    arrays = {n: np.ascontiguousarray(a) for n, a in arrays.items()}
    nc = bacc.Bacc("TRN2", target_bir_lowering=False, num_devices=1)
    args = {n: nc.dram_tensor(n, a.shape, mybir.dt.from_np(a.dtype), kind="ExternalInput").ap()
            for n, a in arrays.items()}
    out = nc.dram_tensor("out", (SEQ, D), F32, kind="ExternalOutput").ap()
    build_kernel(nc, out=out, **args)
    r = run_bass_kernel_spmd(nc, [arrays], core_ids=[0])
    return r.results[0]["out"].reshape(1, SEQ, D)
```
